# Optimizing a Trainium2 kernel written in Bass

```python
import math
import jax, jax.numpy as jnp
from jax import lax
import numpy as np

D_MODEL = 1024
BATCH = 1
SEQ = 512
DEPTH = 2
DEC_BATCH = 1
DEC_SEQ = 64
PAST_LEN = 256

CHUNK = 64
Q_BLOCK = 128
N_MIXERS = 2
N_DIFF_LAYERS = (DEPTH + 1) // 2
N_FOX_LAYERS = DEPTH // 2
DIFF_HEADS = 8
DIFF_QK_DIM = 64
DIFF_V_DIM = 2 * DIFF_QK_DIM
DIFF_QK_WIDTH = 2 * DIFF_HEADS * DIFF_QK_DIM
DIFF_V_WIDTH = DIFF_HEADS * DIFF_V_DIM
FOX_HEADS = 16
FOX_HEAD_DIM = 64
FOX_WIDTH = FOX_HEADS * FOX_HEAD_DIM
D_FF = ((-(-8 * D_MODEL // 3) + 255) // 256) * 256
ROPE_THETA = 10000.0
NORM_EPS = 1e-6
SUBLN_EPS = 1e-5
LAMBDA_STD = 0.1
FORGET_BIAS_MEAN = 2.0

kernel_name = "diff_fox_streaming_encoder_step"

def _rmsnorm(x, w, eps=NORM_EPS):
    xf = x.astype(jnp.float32)
    y = xf * lax.rsqrt(jnp.mean(xf * xf, axis=-1, keepdims=True) + eps)
    return (y * w.astype(jnp.float32)).astype(x.dtype)

def _rope(x, pos):
    half = x.shape[-1] // 2
    inv_freq = ROPE_THETA ** (-jnp.arange(half, dtype=jnp.float32) / half)
    ang = pos.astype(jnp.float32)[:, None] * inv_freq[None, :]
    cos = jnp.cos(ang)[None, :, None, :]
    sin = jnp.sin(ang)[None, :, None, :]
    xf = x.astype(jnp.float32)
    x1, x2 = xf[..., :half], xf[..., half:]
    return jnp.concatenate([x1 * cos - x2 * sin, x2 * cos + x1 * sin], axis=-1).astype(x.dtype)

def _lambda_init(layer):
    return 0.8 - 0.6 * math.exp(-0.3 * layer)

def _swiglu(h, w_in, w_out):
    gate, up = jnp.split(h @ w_in, 2, axis=-1)
    return (jax.nn.silu(gate) * up) @ w_out

def _diff_attend(q, k, v, q_pos, k_pos, lam):
    s = jnp.einsum('bqhd,bkhd->bhqk', q, k, preferred_element_type=jnp.float32) * (DIFF_QK_DIM ** -0.5)
    allowed = (k_pos[None, :] // CHUNK) <= (q_pos[:, None] // CHUNK)
    p = jax.nn.softmax(jnp.where(allowed[None, None], s, -jnp.inf), axis=-1)
    b, _, tq, tk = p.shape
    p = p.reshape(b, DIFF_HEADS, 2, tq, tk)
    a = p[:, :, 0] - lam * p[:, :, 1]
    return jnp.einsum('bhqk,bkhe->bqhe', a.astype(v.dtype), v)

def _fox_attend(q, k, v, cq, ck, q_pos, k_pos):
    s = jnp.einsum('bqhd,bkhd->bhqk', q, k, preferred_element_type=jnp.float32) * (FOX_HEAD_DIM ** -0.5)
    s = s + jnp.transpose(cq, (0, 2, 1))[:, :, :, None] - jnp.transpose(ck, (0, 2, 1))[:, :, None, :]
    allowed = k_pos[None, :] <= q_pos[:, None]
    p = jax.nn.softmax(jnp.where(allowed[None, None], s, -jnp.inf), axis=-1)
    return jnp.einsum('bhqk,bkhd->bqhd', p.astype(v.dtype), v)

def _diff_mixer(h, pos, w_qkv, w_o, lam_params, subln_w, layer, cache_k=None, cache_v=None):
    b, t, _ = h.shape
    qkv = h @ w_qkv
    q = _rope(qkv[..., :DIFF_QK_WIDTH].reshape(b, t, 2 * DIFF_HEADS, DIFF_QK_DIM), pos)
    k = _rope(qkv[..., DIFF_QK_WIDTH:2 * DIFF_QK_WIDTH].reshape(b, t, 2 * DIFF_HEADS, DIFF_QK_DIM), pos)
    v = qkv[..., 2 * DIFF_QK_WIDTH:].reshape(b, t, DIFF_HEADS, DIFF_V_DIM)
    lam_init = _lambda_init(layer)
    lp = lam_params.astype(jnp.float32)
    lam = jnp.exp(jnp.sum(lp[0] * lp[1])) - jnp.exp(jnp.sum(lp[2] * lp[3])) + lam_init
    if cache_k is None:
        outs = [_diff_attend(q[:, lo:lo + Q_BLOCK], k[:, :lo + Q_BLOCK], v[:, :lo + Q_BLOCK],
                             pos[lo:lo + Q_BLOCK], pos[:lo + Q_BLOCK], lam)
                for lo in range(0, t, Q_BLOCK)]
        o = jnp.concatenate(outs, axis=1)
    else:
        p_len = cache_k.shape[1]
        k_all = jnp.concatenate([cache_k.astype(k.dtype), k], axis=1)
        v_all = jnp.concatenate([cache_v.astype(v.dtype), v], axis=1)
        k_pos = jnp.arange(p_len + t, dtype=jnp.int32)
        o = _diff_attend(q, k_all, v_all, pos, k_pos, lam)
    o = _rmsnorm(o, subln_w, SUBLN_EPS) * (1.0 - lam_init)
    return o.reshape(b, t, DIFF_V_WIDTH) @ w_o, k, v

def _fox_mixer(h, pos, w_qkvf, b_f, w_o, cache_k=None, cache_v=None, cache_logf=None):
    b, t, _ = h.shape
    proj = h @ w_qkvf
    q = proj[..., :FOX_WIDTH].reshape(b, t, FOX_HEADS, FOX_HEAD_DIM)
    k = proj[..., FOX_WIDTH:2 * FOX_WIDTH].reshape(b, t, FOX_HEADS, FOX_HEAD_DIM)
    v = proj[..., 2 * FOX_WIDTH:3 * FOX_WIDTH].reshape(b, t, FOX_HEADS, FOX_HEAD_DIM)
    logf = jax.nn.log_sigmoid(proj[..., 3 * FOX_WIDTH:].astype(jnp.float32) + b_f.astype(jnp.float32))
    if cache_k is None:
        c = jnp.cumsum(logf, axis=1)
        outs = [_fox_attend(q[:, lo:lo + Q_BLOCK], k[:, :lo + Q_BLOCK], v[:, :lo + Q_BLOCK],
                            c[:, lo:lo + Q_BLOCK], c[:, :lo + Q_BLOCK],
                            pos[lo:lo + Q_BLOCK], pos[:lo + Q_BLOCK])
                for lo in range(0, t, Q_BLOCK)]
        o = jnp.concatenate(outs, axis=1)
    else:
        p_len = cache_k.shape[1]
        c = jnp.cumsum(jnp.concatenate([cache_logf.astype(jnp.float32), logf], axis=1), axis=1)
        k_all = jnp.concatenate([cache_k.astype(k.dtype), k], axis=1)
        v_all = jnp.concatenate([cache_v.astype(v.dtype), v], axis=1)
        k_pos = jnp.arange(p_len + t, dtype=jnp.int32)
        o = _fox_attend(q, k_all, v_all, c[:, p_len:], c, pos, k_pos)
    return o.reshape(b, t, FOX_WIDTH) @ w_o, k, v, logf

def setup_inputs(seed: int = 0) -> dict:
    key = jax.random.key(seed)
    ks = jax.random.split(key, 20)
    nrm = jax.random.normal
    f32 = jnp.float32
    return {
        "x_prompt": nrm(ks[0], (BATCH, SEQ, D_MODEL), f32),
        "x_sample": nrm(ks[1], (DEC_BATCH, DEC_SEQ, D_MODEL), f32),
        "cache_diff_k": nrm(ks[2], (N_DIFF_LAYERS, DEC_BATCH, PAST_LEN, 2 * DIFF_HEADS, DIFF_QK_DIM), f32),
        "cache_diff_v": nrm(ks[3], (N_DIFF_LAYERS, DEC_BATCH, PAST_LEN, DIFF_HEADS, DIFF_V_DIM), f32),
        "cache_fox_k": nrm(ks[4], (N_FOX_LAYERS, DEC_BATCH, PAST_LEN, FOX_HEADS, FOX_HEAD_DIM), f32),
        "cache_fox_v": nrm(ks[5], (N_FOX_LAYERS, DEC_BATCH, PAST_LEN, FOX_HEADS, FOX_HEAD_DIM), f32),
        "cache_fox_logf": jax.nn.log_sigmoid(FORGET_BIAS_MEAN + nrm(ks[6], (N_FOX_LAYERS, DEC_BATCH, PAST_LEN, FOX_HEADS), f32)),
        "norm_mix": 1.0 + 0.02 * nrm(ks[7], (DEPTH, D_MODEL), f32),
        "norm_ffn": 1.0 + 0.02 * nrm(ks[8], (DEPTH, D_MODEL), f32),
        "norm_final": 1.0 + 0.02 * nrm(ks[9], (D_MODEL,), f32),
        "diff_w_qkv": nrm(ks[10], (N_DIFF_LAYERS, D_MODEL, 2 * DIFF_QK_WIDTH + DIFF_V_WIDTH), f32) * D_MODEL ** -0.5,
        "diff_w_o": nrm(ks[11], (N_DIFF_LAYERS, DIFF_V_WIDTH, D_MODEL), f32) * DIFF_V_WIDTH ** -0.5,
        "diff_lambda": LAMBDA_STD * nrm(ks[12], (N_DIFF_LAYERS, 4, DIFF_QK_DIM), f32),
        "diff_subln": 1.0 + 0.02 * nrm(ks[13], (N_DIFF_LAYERS, DIFF_V_DIM), f32),
        "fox_w_qkvf": nrm(ks[14], (N_FOX_LAYERS, D_MODEL, 3 * FOX_WIDTH + FOX_HEADS), f32) * D_MODEL ** -0.5,
        "fox_b_f": FORGET_BIAS_MEAN + 0.5 * nrm(ks[15], (N_FOX_LAYERS, FOX_HEADS), f32),
        "fox_w_o": nrm(ks[16], (N_FOX_LAYERS, FOX_WIDTH, D_MODEL), f32) * FOX_WIDTH ** -0.5,
        "ffn_w_in": nrm(ks[17], (DEPTH, D_MODEL, 2 * D_FF), f32) * D_MODEL ** -0.5,
        "ffn_w_out": nrm(ks[18], (DEPTH, D_FF, D_MODEL), f32) * D_FF ** -0.5,
    }

def reference(x_prompt, x_sample, cache_diff_k, cache_diff_v, cache_fox_k, cache_fox_v, cache_fox_logf,
              norm_mix, norm_ffn, norm_final, diff_w_qkv, diff_w_o, diff_lambda, diff_subln,
              fox_w_qkvf, fox_b_f, fox_w_o, ffn_w_in, ffn_w_out):
    s_len = x_prompt.shape[1]
    t_len = x_sample.shape[1]
    p_len = cache_diff_k.shape[2]
    pos_p = jnp.arange(s_len, dtype=jnp.int32)
    pos_s = p_len + jnp.arange(t_len, dtype=jnp.int32)
    xp, xs = x_prompt, x_sample
    dk_p, dv_p, fk_p, fv_p, fl_p = [], [], [], [], []
    dk_s, dv_s, fk_s, fv_s, fl_s = [], [], [], [], []
    for i in range(DEPTH):
        j = i // N_MIXERS
        hp = _rmsnorm(xp, norm_mix[i])
        hs = _rmsnorm(xs, norm_mix[i])
        if i % N_MIXERS == 0:
            yp, kp, vp = _diff_mixer(hp, pos_p, diff_w_qkv[j], diff_w_o[j], diff_lambda[j], diff_subln[j], i)
            ys, ks_, vs_ = _diff_mixer(hs, pos_s, diff_w_qkv[j], diff_w_o[j], diff_lambda[j], diff_subln[j], i,
                                       cache_diff_k[j], cache_diff_v[j])
            dk_p.append(kp); dv_p.append(vp); dk_s.append(ks_); dv_s.append(vs_)
        else:
            yp, kp, vp, lp = _fox_mixer(hp, pos_p, fox_w_qkvf[j], fox_b_f[j], fox_w_o[j])
            ys, ks_, vs_, ls_ = _fox_mixer(hs, pos_s, fox_w_qkvf[j], fox_b_f[j], fox_w_o[j],
                                           cache_fox_k[j], cache_fox_v[j], cache_fox_logf[j])
            fk_p.append(kp); fv_p.append(vp); fl_p.append(lp)
            fk_s.append(ks_); fv_s.append(vs_); fl_s.append(ls_)
        xp = xp + yp
        xs = xs + ys
        xp = xp + _swiglu(_rmsnorm(xp, norm_ffn[i]), ffn_w_in[i], ffn_w_out[i])
        xs = xs + _swiglu(_rmsnorm(xs, norm_ffn[i]), ffn_w_in[i], ffn_w_out[i])
    y_prompt = _rmsnorm(xp, norm_final)
    y_sample = _rmsnorm(xs, norm_final)
    return (y_prompt, y_sample,
            jnp.stack(dk_p), jnp.stack(dv_p), jnp.stack(fk_p), jnp.stack(fv_p), jnp.stack(fl_p),
            jnp.stack(dk_s), jnp.stack(dv_s), jnp.stack(fk_s), jnp.stack(fv_s), jnp.stack(fl_s))


_drawn_inputs = setup_inputs


def setup_inputs(seed=0):
    import zlib

    import numpy as np

    out = dict(_drawn_inputs(seed))
    spreads = {}
    factors = {'cache_fox_logf': 28.776,
     'norm_ffn': 3.35,
     'norm_final': 8.126,
     'diff_subln': 3.612,
     'cache_fox_k': 6.794,
     'cache_fox_v': 4.568}
    for name, (base, spread) in spreads.items():
        noise = np.random.default_rng([zlib.crc32(name.encode()), seed]).standard_normal(out[name].shape)
        drawn = base * np.exp(spread * noise) if base else spread * noise
        out[name] = __import__('jax').numpy.asarray(drawn.astype(out[name].dtype))
    for name, factor in factors.items():
        out[name] = (out[name] * factor).astype(out[name].dtype)
    return out
```

```python
from contextlib import ExitStack

import concourse.bass as bass
from concourse import mybir

F32 = mybir.dt.float32
F32R = mybir.dt.float32r
BF16 = mybir.dt.bfloat16
ALU = mybir.AluOpType
ACT = mybir.ActivationFunctionType
AX_X = mybir.AxisListType.X

P = 128
D = 1024
KT = D // P
SEQ, NEW, PAST = 512, 64, 256
T = SEQ + NEW
HALF = T // 2
TQ = SEQ + P
TK = SEQ + P + PAST
G = 8
F = 2816
FT = F // P
OUT_PARTS = (8, 8, 6)
U_WO, U_IN, U_OUT, U_LAYER = 24, 32, 76, 100
N_WO, N_IN, N_OUT, N_LAYER = 24, 32, 76, 84
SLOTS = 24
QK_SCALE = 0.125
EPS, SUB_EPS = 1e-6, 1e-5
LAM_INIT = 0.2
DIFF, FOX = 0, 1

JOBS = {DIFF: [(i, h) for i in (4, 3, 2, 1, 0) for h in (0, 1)],
        FOX: [(i, h) for h in (0, 1) for i in (4, 3, 2, 1, 0)]}
S_AT = {DIFF: [0, 0, 3, 4, 7, 8, 11, 12, 15, 16], FOX: [0, 1, 3, 5, 8, 10, 12, 14, 16, 18]}
T_AT = {DIFF: [5, 9, 13, 17, 20], FOX: [4, 6, 8, 10, 12, 14, 16, 18, 20, 21]}
PVS_AT = {DIFF: [9], FOX: [9, 17]}
PVP_AT = {DIFF: [23], FOX: [14, 23]}
VT_AT, SS_AT = 2, 4


class Num:

    def __init__(self, c, k=0, it=None):
        self.c, self.k, self.it = c, k, it

    def __add__(self, n):
        return Num(self.c + n, self.k, self.it)

    def __sub__(self, n):
        return self + (-n)

    def __mul__(self, n):
        return Num(self.c * n, self.k * n, self.it)

    def half(self):
        assert self.k % 2 == 0
        return Num(self.c // 2, self.k // 2, self.it)

    def v(self):
        return self.c if self.it is None or self.k == 0 else self.it * self.k + self.c


def val(n):
    n = n if isinstance(n, Num) else Num(n)
    assert n.c > 0, n.c
    return n.v()


def some(n):
    return n > 0 if isinstance(n, int) else n.c > 0 or n.it is not None


def later(g):
    return some(g)


def at(tile, i):
    if i.it is None or i.k == 0:
        return tile[:, i.c, :]
    return tile[:, bass.ds(i.v(), 1), :].rearrange("p a b -> p (a b)")


def width(i):
    return 3 * P if i == 4 else (i + 1) * P


def encoder(nc, w_units, w_forget, x_in, small, cst, cst16, rope_tab, k_past, v_past, f_past,
            y_out, dk_out, dv_out, fk_out, fv_out, lf_out):
    k_out = (dk_out, fk_out)
    v_out = (dv_out, fv_out)
    with ExitStack() as ctx:
        def sb(name, shape, dt=F32):
            return ctx.enter_context(nc.sbuf_tensor(name, shape, dt))

        def sem(name):
            return ctx.enter_context(nc.semaphore(name))

        xT = sb("xT", [P, KT, T])
        xh = sb("xh", [P, KT, T], F32R)
        xl = sb("xl", [P, KT, T], F32R)
        w_raw = [sb(f"w_raw{s}", [P, KT, P]) for s in range(2)]
        w_hi = [sb(f"w_hi{s}", [P, KT, P], F32R) for s in range(2)]
        w_lo = [sb(f"w_lo{s}", [P, KT, P], F32R) for s in range(2)]
        rs = sb("rs", [P, T])
        acc = sb("acc", [P, T])
        smalls = sb("smalls", [P, 5 * KT + 2 + 2 * P])
        norm_w = [smalls[:, KT * i:KT * (i + 1)] for i in range(5)]
        c0 = 5 * KT
        subln, b_f, lam_p = smalls[:, c0:c0 + 1], smalls[:, c0 + 1:c0 + 2], smalls[:, c0 + 2:c0 + 2 + 2 * P]
        cstf = sb("cstf", [P, 2 * P + 2 * G])
        ident, ones, head_sel = cstf[:, 0:P], cstf[:, P:2 * P], cstf[:, 2 * P:2 * P + 2 * G]
        csth = sb("csth", [P, 3 * P], BF16)
        ident16, mask = csth[:, 0:P], (csth[:, P:2 * P], csth[:, 2 * P:3 * P])
        eps = sb("eps", [P, 2])
        nlam = sb("nlam", [P, 8])
        sub_w = sb("sub_w", [P, 1])
        nmax = sb("nmax", [P, 4])
        den = sb("den", [P, 4])
        rden = sb("rden", [P, 4])
        nlr = sb("nlr", [P, 4])

        ARENA = 122112
        arena_start = -(-nc.sbuf_base // 32) * 32
        assert arena_start + ARENA <= nc.sbuf_usable_end
        holder = {"at": 0}

        def place(name, shape, dt=F32, offset=None):
            n = 4
            for s in shape[1:]:
                n *= s
            if offset is None:
                offset = holder["at"]
                holder["at"] += n
            assert offset + n <= ARENA, name
            return nc.alloc_sbuf_tensor_at(name, shape, dt, offset=arena_start + offset)

        qh = [place(f"qh{s}", [P, TQ], F32R) for s in range(2)]
        ql = [place(f"ql{s}", [P, TQ], F32R) for s in range(2)]
        kh = [place(f"kh{s}", [P, TK], F32R) for s in range(2)]
        kl = [place(f"kl{s}", [P, TK], F32R) for s in range(2)]
        qf = place("qf", [P, T])
        kf = place("kf", [P, TK])
        vf = place("vf", [P, TQ])
        vr = place("vr", [P, 7, P])
        vh = place("vh", [P, 7, P], F32R)
        vl = place("vl", [P, 7, P], F32R)
        pr = place("pr", [P, 4, SEQ])
        pt_at = holder["at"]
        pth = place("pth", [P, 4, SEQ], F32R)
        ptl = place("ptl", [P, 4, SEQ], F32R)
        psh = place("psh", [P, 3, P], F32R)
        psl = place("psl", [P, 3, P], F32R)
        o_at = holder["at"]
        oh = place("oh", [P, G, T], F32R)
        ol = place("ol", [P, G, T], F32R)
        own_at = holder["at"]
        cosr = place("cosr", [P, T])
        sinr = place("sinr", [P, T])
        qsw = place("qsw", [P, T])
        og = place("og", [P, T])
        osq = place("osq", [P, T])
        ors = place("ors", [P, T])
        holder["at"] = own_at
        aug_m = place("aug_m", [P, TQ])
        aug_r = place("aug_r", [P, TK], F32R)
        aug_l = [place(f"aug_l{h}", [P, TQ], F32R) for h in range(2)]
        holder["at"] = pt_at
        f_raw = place("f_raw", [P, KT, P])
        f_hi = place("f_hi", [P, KT, P], F32R)
        f_lo = place("f_lo", [P, KT, P], F32R)
        holder["at"] = o_at
        fz = place("fz", [P, T])
        fe = place("fe", [P, T])
        lf = place("lf", [P, TQ])
        lft = place("lft", [P, 7, P])
        cum = place("cum", [P, TK])
        cumh = place("cumh", [P, TK], F32R)
        upper = place("upper", [P, SEQ])
        holder["at"] = 0
        hh = place("hh", [P, FT, T], F32R)
        hl = place("hl", [P, FT, T], F32R)
        gf = place("gf", [P, T])
        sg = place("sg", [P, T])
        uf = place("uf", [P, T])
        hf = place("hf", [P, T])
        sqt = place("sqt", [P, T], offset=ARENA - 4 * T)
        yt = place("yt", [P, KT, T], offset=0)

        ps = ctx.enter_context(nc.psum_tensor("ps", [P, 4, 512], F32))
        sps = ctx.enter_context(nc.psum_tensor("sps", [P, 2, 512], F32))
        tps = ctx.enter_context(nc.psum_tensor("tps", [P, 4, P], F32))
        ops = ctx.enter_context(nc.psum_tensor("ops", [P, 512], F32))

        def proj(n2):
            return ps[:, 2 * n2:2 * n2 + 2, 0:HALF]

        def halves(ap):
            return ap.rearrange("p (a b) -> p a b", a=2)

        x_loaded = [sem(f"x_loaded{k}") for k in range(KT)]
        cst_loaded = sem("cst_loaded")
        rope_loaded = sem("rope_loaded")
        w_loaded = [sem(f"w_loaded{s}") for s in range(2)]
        f_loaded = sem("f_loaded")
        upper_loaded = sem("upper_loaded")
        fpast_loaded = sem("fpast_loaded")
        kpast_loaded = sem("kpast_loaded")
        vpast_loaded = sem("vpast_loaded")
        k_stored = sem("k_stored")
        v_stored = sem("v_stored")
        lf_stored = sem("lf_stored")
        y_stored = sem("y_stored")
        w_hi_done = sem("w_hi_done")
        w_lo_done = sem("w_lo_done")
        w_used = sem("w_used")
        ps_read = sem("ps_read")
        ps_swapped = sem("ps_swapped")
        xh_done = sem("xh_done")
        xl_done = sem("xl_done")
        sq_done = sem("sq_done")
        acc_done = sem("acc_done")
        acc_zero = sem("acc_zero")
        ss_done = sem("ss_done")
        ln_done = sem("ln_done")
        r_ready = sem("r_ready")
        pads_zero = sem("pads_zero")
        eps_set = sem("eps_set")
        lam_step = sem("lam_step")
        lam_exp = sem("lam_exp")
        rope_scaled = sem("rope_scaled")
        part_done = sem("part_done")
        rope_done = sem("rope_done")
        kh_done = sem("kh_done")
        kl_done = sem("kl_done")
        qh_done = sem("qh_done")
        ql_done = sem("ql_done")
        vt_done = sem("vt_done")
        vr_done = sem("vr_done")
        vh_done = sem("vh_done")
        vl_done = sem("vl_done")
        s_done = sem("s_done")
        max_done = sem("max_done")
        exp_done = sem("exp_done")
        rden_done = sem("rden_done")
        nlr_done = sem("nlr_done")
        pa_done = sem("pa_done")
        p_ready = sem("p_ready")
        t_done = sem("t_done")
        pt_hi = sem("pt_hi")
        pt_lo = sem("pt_lo")
        pvs_done = sem("pvs_done")
        pvp_done = sem("pvp_done")
        os_hi = sem("os_hi")
        os_lo = sem("os_lo")
        op_hi = sem("op_hi")
        op_lo = sem("op_lo")
        osq_done = sem("osq_done")
        oss_done = sem("oss_done")
        oln_done = sem("oln_done")
        ors_done = sem("ors_done")
        on_done = sem("on_done")
        oh_done = sem("oh_done")
        ol_done = sem("ol_done")
        aug_l_done = sem("aug_l_done")
        f_hi_done = sem("f_hi_done")
        f_lo_done = sem("f_lo_done")
        f_proj = sem("f_proj")
        f_step = sem("f_step")
        f_exp = sem("f_exp")
        f_ln = sem("f_ln")
        f_tr = sem("f_tr")
        f_lt = sem("f_lt")
        f_cum = sem("f_cum")
        cum_hi = sem("cum_hi")
        sg_done = sem("sg_done")
        hf_done = sem("hf_done")
        hh_done = sem("hh_done")
        hl_done = sem("hl_done")
        y_done = sem("y_done")

        def t_index(L, a, jj):
            return a * 5 + jj if L == DIFF else a * 10 + (5 * G + jj)

        def v_index(L, a, h):
            return a if L == DIFF else a * 2 + (G + h)

        def prep_count(L, ffn, k):
            return KT * (2 * L + ffn) + k

        block = ctx.enter_context(nc.Block())

        @block.sync
        def _(sp):
            def load_unit(u, cols=KT):
                slot = u.c % 2
                if some(u - 1):
                    sp.wait_ge(w_hi_done, val(u - 1))
                if some(u - 1):
                    sp.wait_ge(w_lo_done, val(u - 1))
                if u.it is None or u.k == 0:
                    src = w_units[u.c]
                else:
                    src = w_units[bass.ds(u.v(), 1)].rearrange("a p n -> (a p) n")
                sp.dma_start(w_raw[slot][:, 0:cols, :], src[:, 0:cols * P].rearrange("p (k n) -> p k n", n=P)
                             ).then_inc(w_loaded[slot], 16)

            def rows(dram, g):
                if g.it is None or g.k == 0:
                    return dram[P * g.c:P * (g.c + 1), :]
                return dram[bass.ds((g * P).v(), P), :]

            def store_v(L, g):
                sp.wait_ge(ps_read, val(g * 3 + (N_LAYER * L + 3)))
                sp.dma_start(rows(v_out[L], g), vf[:, 0:T]).then_inc(v_stored, 16)

            def store_k(L, g):
                if L == DIFF:
                    sp.wait_ge(rope_done, val(g * 2 + 1))
                else:
                    sp.wait_ge(ps_read, val(g * 3 + (N_LAYER * L + 1)))
                sp.dma_start(rows(k_out[L], g), kf[:, 0:T]).then_inc(k_stored, 16)

            def load_vpast(L, g):
                if some(g + G * L):
                    sp.wait_ge(vh_done, val(g + G * L))
                if some(g + G * L):
                    sp.wait_ge(vl_done, val(g + G * L))
                if g.it is None or g.k == 0:
                    src = v_past[L * G + g.c]
                else:
                    src = v_past[bass.ds((g + L * G).v(), 1)].rearrange("a p n -> (a p) n")
                sp.dma_start(vr[:, 5:7, :], src.rearrange("p (b n) -> p b n", b=2)).then_inc(vpast_loaded, 16)

            def load_kpast(L, g):
                if some(g + G * L):
                    sp.wait_ge(kh_done, val(g + G * L))
                if some(g + G * L):
                    sp.wait_ge(kl_done, val(g + G * L))
                sp.dma_start(kf[:, TQ:TK], rows(k_past, g + L * G)).then_inc(kpast_loaded, 16)

            def group(L, g, first=False, second=False):
                u = g * 3 + U_LAYER * L
                load_unit(u)
                if not first:
                    if not second:
                        store_v(L, g - 2)
                    load_vpast(L, g - 1)
                if second and L == FOX:
                    sp.wait_ge(f_step, 5)
                    sp.dma_start(lf_out, lf[0:2 * G, 0:T]).then_inc(lf_stored, 16)
                load_unit(u + 1)
                if not first:
                    store_k(L, g - 1)
                elif L == FOX:
                    sp.wait_ge(w_used, val(U_LAYER))
                    sp.dma_start(f_raw[:], w_forget.rearrange("p (k n) -> p k n", n=P)).then_inc(f_loaded, 16)
                    sp.dma_start(upper[:], cst[:, 2 * P + 2 * G:]).then_inc(upper_loaded, 16)
                    sp.dma_start(lft[:, 5:7, :], f_past.rearrange("p (b n) -> p b n", b=2)).then_inc(fpast_loaded, 16)
                load_kpast(L, g)
                load_unit(u + 2)

            for k in range(KT):
                sp.dma_start(xT[:, k, :], x_in[P * k:P * (k + 1), :]).then_inc(x_loaded[k], 16)
                if k == 0:
                    sp.dma_start(smalls[:], small).then_inc(cst_loaded, 16)
                    sp.dma_start(cstf[:], cst[:, 0:2 * P + 2 * G]).then_inc(cst_loaded, 16)
                    sp.dma_start(csth[:], cst16).then_inc(cst_loaded, 16)
            sp.dma_start(cosr[:], rope_tab[:, 0:T]).then_inc(rope_loaded, 16)
            sp.dma_start(sinr[:], rope_tab[:, T:2 * T]).then_inc(rope_loaded, 16)
            for L in (DIFF, FOX):
                group(L, Num(0), first=True)
                group(L, Num(1), second=True)
                with sp.Fori(0, 3) as it:
                    for par in range(2):
                        group(L, Num(2 + par, 2, it))
                for n in range(KT):
                    load_unit(Num(U_LAYER * L + U_WO + n))
                    if n == 0:
                        store_v(L, Num(6))
                        load_vpast(L, Num(7))
                    if n == 1:
                        store_k(L, Num(7))
                    if n == 2:
                        store_v(L, Num(7))
                with sp.Fori(0, FT) as it:
                    for s in range(2):
                        load_unit(Num(U_LAYER * L + U_IN + s, 2, it))
                with sp.Fori(0, KT // 2) as it:
                    for s in range(6):
                        load_unit(Num(U_LAYER * L + U_OUT + s, 6, it), OUT_PARTS[s % 3])
            for k in range(KT):
                sp.wait_ge(y_done, val(k + 1))
                sp.dma_start(y_out[P * k:P * (k + 1), :], yt[:, k, :]).then_inc(y_stored, 16)
            sp.wait_ge(y_stored, 16 * KT)
            sp.wait_ge(k_stored, 16 * 2 * G)
            sp.wait_ge(v_stored, 16 * 2 * G)
            sp.wait_ge(lf_stored, 16)

        @block.tensor
        def _(pe):
            def slice_(u, n, k, rhs_hi, rhs_lo, kt, start, stop):
                slot, out = u.c % 2, proj(n.c % 2)
                for w, rhs in ((w_hi[slot], rhs_hi), (w_hi[slot], rhs_lo), (w_lo[slot], rhs_hi)):
                    for half in range(2):
                        mm = nc.tensor.matmul(out[:, half, :], w[:, k, :], rhs[:, kt, half * HALF:(half + 1) * HALF],
                                              start=start and w is w_hi[slot] and rhs is rhs_hi,
                                              stop=stop and w is w_lo[slot])
                return mm

            def open_unit(u, n=None, tile=True, swapped=None):
                pe.wait_ge(w_hi_done, val(u + 1))
                pe.wait_ge(w_lo_done, val(u + 1))
                if tile:
                    if some(n - 1):
                        pe.wait_ge(ps_read, val(n - 1))
                    if swapped is not None:
                        pe.wait_ge(ps_swapped, val(swapped))

            def norm_sum(i):
                pe.wait_ge(acc_done, val(KT * (i + 1)))
                for half in range(2):
                    mm = nc.tensor.matmul(sps[:, half, 0:HALF], ones, acc[:, half * HALF:(half + 1) * HALF],
                                          start=True, stop=True)
                mm.then_inc(ss_done, 1)

            def first_unit(u, n, prep, norm):
                open_unit(u, n)
                for k in range(KT):
                    pe.wait_ge(xh_done, val(prep + k + 1))
                    pe.wait_ge(xl_done, val(prep + k + 1))
                    if k == 6:
                        norm_sum(norm)
                    mm = slice_(u, n, k, xh, xl, k, k == 0, k == KT - 1)
                return mm

            def score(L, a, par, jj):
                i, h = JOBS[L][jj]
                J = (a + G * L) * 10 + jj
                b = slice(64 * h, 64 * h + 64)
                out = sps[:, jj % 2, 0:width(i)]
                q = slice(P * i, P * i + P)
                k = slice(SEQ, TK) if i == 4 else slice(0, width(i))
                if some(J - 1):
                    pe.wait_ge(exp_done, val(J - 1))
                if jj == 0:
                    for s in (qh_done, ql_done, kh_done, kl_done):
                        pe.wait_ge(s, val(a + (G * L + 1)))
                pe_mm = nc.tensor.matmul
                pe_mm(out, qh[par][b, q], kh[par][b, k], start=True, stop=False)
                pe_mm(out, ql[par][b, q], kh[par][b, k], start=False, stop=False)
                pe_mm(out, qh[par][b, q], kl[par][b, k], start=False, stop=False)
                if L == FOX:
                    pe.wait_ge(aug_l_done, val(a * 2 + (h + 1)))
                    pe_mm(out, aug_l[h][:, q], aug_r[:, k], start=False, stop=False)
                d = 0 if i == 4 else i
                pe_mm(sps[:, jj % 2, P * d:P * d + P], ident16, mask[L], start=False, stop=True
                      ).then_inc(s_done, 1)

            def transpose_p(L, a, par, tt):
                jj = 2 * tt if L == DIFF else tt
                i, h = JOBS[L][jj]
                tau = t_index(L, a, tt)
                slot = (10 * par + jj) % 4
                pe.wait_ge(p_ready, val(tau + 1))
                if some(tau):
                    pe.wait_ge(pt_lo, val(tau))
                for b in range(width(i) // P):
                    mm = nc.tensor.transpose(tps[:, b, :], pr[:, slot, P * b:P * b + P], ident)
                mm.then_inc(t_done, 1)

            def transpose_v(L, a):
                pe.wait_ge(ps_read, val(a * 3 + (N_LAYER * L + 3)))
                if some(t_index(L, a, 0)):
                    pe.wait_ge(pt_lo, val(t_index(L, a, 0)))
                if some(v_index(L, a, 0)):
                    pe.wait_ge(op_hi, val(v_index(L, a, 0)))
                if L == FOX:
                    if some(a * 2):
                        pe.wait_ge(op_lo, val(a * 2))
                for b in range(4):
                    nc.tensor.transpose(tps[:, b, :], vf[:, P * b:P * b + P], ident)
                nc.tensor.transpose(ops[:, 0:P], vf[:, SEQ:TQ], ident).then_inc(vt_done, 1)

            def pv_sample(L, a, h):
                tt = 0 if L == DIFF else 5 * h
                pe.wait_ge(pt_lo, val(t_index(L, a, tt) + 1))
                pe.wait_ge(vh_done, val(a + (G * L + 1)))
                pe.wait_ge(vl_done, val(a + (G * L + 1)))
                if some(v_index(L, a, h)):
                    pe.wait_ge(op_hi, val(v_index(L, a, h)))
                if L == FOX:
                    if some(a * 2 + h):
                        pe.wait_ge(op_lo, val(a * 2 + h))
                elif later(a):
                    pe.wait_ge(oln_done, val(a))
                for b, blk in enumerate((4, 5, 6)):
                    for v, p in ((vh, psh), (vh, psl), (vl, psh)):
                        mm = nc.tensor.matmul(ops[:, 0:NEW], v[:, blk, :], p[:, b, 0:NEW],
                                              start=b == 0 and v is vh and p is psh, stop=b == 2 and v is vl)
                mm.then_inc(pvs_done, 1)

            def pv_prompt(L, a, h):
                tt = 4 if L == DIFF else 5 * h + 4
                pe.wait_ge(pt_lo, val(t_index(L, a, tt) + 1))
                pe.wait_ge(os_hi, val(v_index(L, a, h) + 1))
                if L == FOX:
                    pe.wait_ge(os_lo, val(a * 2 + (h + 1)))
                for j in range(4):
                    for v, p in ((vh, pth), (vh, ptl), (vl, pth)):
                        mm = nc.tensor.matmul(ops[:, P * j:SEQ], v[:, j, :], p[:, j, P * j:SEQ],
                                              start=j == 0 and v is vh and p is pth, stop=j == 3 and v is vl)
                mm.then_inc(pvp_done, 1)

            def head_norm_sum(a):
                pe.wait_ge(osq_done, val(a + 1))
                nc.tensor.matmul(ops[:], ones, osq[:, 0:SEQ], start=True, stop=True)
                nc.tensor.matmul(tps[:, 0, 0:NEW], ones, osq[:, SEQ:T], start=True, stop=True).then_inc(oss_done, 1)

            def attention(L, a, par, slot, first=False):
                if slot == VT_AT:
                    transpose_v(L, a)
                if slot == SS_AT and L == DIFF and not first:
                    pe.wait_ge(vr_done, val((a + 1) * 2))
                    head_norm_sum(a - 1)
                for jj in range(10):
                    if S_AT[L][jj] == slot:
                        score(L, a, par, jj)
                for tt in range(len(T_AT[L])):
                    if T_AT[L][tt] == slot:
                        if tt == 0:
                            pe.wait_ge(vr_done, val((a + (G * L + 1)) * 2))
                            if L == DIFF and not first:
                                pe.wait_ge(oln_done, val(a))
                        transpose_p(L, a, par, tt)
                for h in range(len(PVS_AT[L])):
                    if PVS_AT[L][h] == slot:
                        pv_sample(L, a, h)
                    if PVP_AT[L][h] == slot:
                        pv_prompt(L, a, h)

            def group(L, g, par, first=False):
                u, n = g * 3 + U_LAYER * L, g * 3 + N_LAYER * L
                for slot in range(SLOTS):
                    attention(L, g - 1, 1 - par, slot, first)
                    part, k = slot // KT, slot % KT
                    if k == 0:
                        swapped = None
                        if L == DIFF:
                            swapped = (g * 2, g * 2, g * 2 + 1)[part]
                        open_unit(u + part, n + part, swapped=swapped)
                    mm = slice_(u + part, n + part, k, xh, xl, k, k == 0, k == KT - 1)
                    if k == KT - 1:
                        mm.then_inc(w_used, 1)

            def first_group(L):
                u, n = Num(U_LAYER * L), Num(N_LAYER * L)
                first_unit(u, n, prep_count(L, 0, 0), 2 * L).then_inc(w_used, 1)
                if L == FOX:
                    pe.wait_ge(f_hi_done, 1)
                    pe.wait_ge(f_lo_done, 1)
                    pe.wait_ge(r_ready, 3)
                    for k in range(KT):
                        for w, rhs in ((f_hi, xh), (f_hi, xl), (f_lo, xh)):
                            for half in range(2):
                                mm = nc.tensor.matmul(sps[:, half, 0:HALF], w[:, k, :],
                                                      rhs[:, k, half * HALF:(half + 1) * HALF],
                                                      start=k == 0 and w is f_hi and rhs is xh,
                                                      stop=k == KT - 1 and w is f_lo)
                    mm.then_inc(f_proj, 1)
                for part in (1, 2):
                    if part == 2 and L == FOX:
                        forget_cumsum()
                    open_unit(u + part, n + part, swapped=1 if L == DIFF and part == 2 else None)
                    for k in range(KT):
                        mm = slice_(u + part, n + part, k, xh, xl, k, k == 0, k == KT - 1)
                    mm.then_inc(w_used, 1)

            def forget_cumsum():
                pe.wait_ge(f_step, 5)
                for b in range(4):
                    nc.tensor.transpose(tps[:, b, :], lf[:, P * b:P * b + P], ident)
                nc.tensor.transpose(ops[:, 0:P], lf[:, SEQ:TQ], ident).then_inc(f_tr, 1)
                pe.wait_ge(f_lt, 2)
                pe.wait_ge(fpast_loaded, 16)
                pe.wait_ge(upper_loaded, 16)
                for b in range(4):
                    nc.tensor.matmul(sps[:, 0, P * b:SEQ], lft[:, b, :], upper[:, 0:SEQ - P * b],
                                     start=b == 0, stop=b == 3)
                for b, blk in enumerate((5, 6, 4)):
                    mm = nc.tensor.matmul(sps[:, 1, P * b:3 * P], lft[:, blk, :], upper[:, 0:3 * P - P * b],
                                          start=b == 0, stop=b == 2)
                mm.then_inc(f_cum, 1)

            def last_attention(L, par):
                a = Num(7)
                u, n = Num(U_LAYER * L + U_WO), Num(N_LAYER * L + N_WO)
                todo = [(0, k) for k in range(6)] + [(1, k) for k in range(6)] + [(0, 6), (1, 6)]
                fill_at = [0, 1, 2, 4, 5, 7, 8, 10, 11, 13, 14, 16, 17, 19]

                def o_ready(g):
                    if L == DIFF:
                        pe.wait_ge(oh_done, val(g + 1))
                        pe.wait_ge(ol_done, val(g + 1))
                    else:
                        pe.wait_ge(op_lo, val(2 * g + 2))

                def one(part, k):
                    if k == 0:
                        open_unit(u + part, n + part,
                                  swapped=2 * G if L == DIFF else None)
                    if part == 0 or k == 7:
                        o_ready(k)
                    return slice_(u + part, n + part, k, oh, ol, k, k == 0, k == KT - 1)

                for slot in range(SLOTS):
                    attention(L, a, par, slot)
                    if slot in fill_at:
                        one(*todo[fill_at.index(slot)])
                if L == DIFF:
                    head_norm_sum(a)
                for part in range(2):
                    mm = one(part, 7)
                    mm.then_inc(w_used, 1)

            for L in (DIFF, FOX):
                first_group(L)
                group(L, Num(1), 1, first=True)
                with pe.Fori(0, 3) as it:
                    for par in range(2):
                        group(L, Num(2 + par, 2, it), par)
                last_attention(L, 1)
                with pe.Fori(0, 3) as it:
                    for s in range(2):
                        u, n = Num(U_LAYER * L + U_WO + 2 + s, 2, it), Num(N_LAYER * L + N_WO + 2 + s, 2, it)
                        open_unit(u, n)
                        for k in range(KT):
                            mm = slice_(u, n, k, oh, ol, k, k == 0, k == KT - 1)
                        mm.then_inc(w_used, 1)
                u, n = Num(U_LAYER * L + U_IN), Num(N_LAYER * L + N_IN)
                first_unit(u, n, prep_count(L, 1, 0), 2 * L + 1).then_inc(w_used, 1)
                open_unit(u + 1, n + 1)
                for k in range(KT):
                    mm = slice_(u + 1, n + 1, k, xh, xl, k, k == 0, k == KT - 1)
                mm.then_inc(w_used, 1)
                with pe.Fori(0, FT - 1) as it:
                    for s in range(2):
                        ui, ni = Num(u.c + 2 + s, 2, it), Num(n.c + 2 + s, 2, it)
                        open_unit(ui, ni)
                        for k in range(KT):
                            mm = slice_(ui, ni, k, xh, xl, k, k == 0, k == KT - 1)
                        mm.then_inc(w_used, 1)

                def out_tile(u, n, first):
                    for part, kts in enumerate(OUT_PARTS):
                        open_unit(u + part, n, tile=part == 0)
                        for k in range(kts):
                            kt = KT * part + k
                            if first:
                                pe.wait_ge(hl_done, val(FT * L + kt + 1))
                            mm = slice_(u + part, n, k, hh, hl, kt, kt == 0, kt == FT - 1)
                        mm.then_inc(w_used, 1)

                u, n = Num(U_LAYER * L + U_OUT), Num(N_LAYER * L + N_OUT)
                out_tile(u, n, True)
                out_tile(u + 3, n + 1, False)
                with pe.Fori(0, 3) as it:
                    for s in range(2):
                        out_tile(Num(u.c + 6 + 3 * s, 6, it), Num(n.c + 2 + s, 2, it), False)
            norm_sum(4)

        def unit_done(L, n):
            return n + U_LAYER * L + 1

        @block.scalar
        def _(act):
            def apart():
                act.wait_ge(cst_loaded, 48)

            def split(u, kts=KT):
                slot = u.c % 2
                act.wait_ge(w_loaded[slot], val((u.half() + 1) * 16))
                if some(u - 1):
                    act.wait_ge(w_used, val(u - 1))
                nc.scalar.activation(w_hi[slot][:, 0:kts, :], w_raw[slot][:, 0:kts, :], ACT.Copy
                                     ).then_inc(w_hi_done, 1)

            def lead(u, kts=KT):
                split(u + 1, kts)

            def column(tile, n):
                if n.it is None or n.k == 0:
                    return tile[:, n.c:n.c + 1]
                return tile[:, bass.ds(n.v(), 1)]

            def prep(i, n):
                if n.it is not None:
                    act.wait_ge(acc_done, val(n + KT * i))
                    apart()
                if i < 4:
                    nc.scalar.activation(at(xh, n), at(xT, n), ACT.Copy, scale=column(norm_w[i], n)
                                         ).then_inc(xh_done, 1)
                if n.it is None:
                    if some(n + KT * i):
                        act.wait_ge(acc_done, val(n + KT * i))
                nc.scalar.activation(sqt[:], at(xT, n), ACT.Square).then_inc(sq_done, 1)

            def scale_of_norm(i):
                act.wait_ge(ss_done, val(i + 1))
                nc.scalar.activation(halves(rs[:]), sps[:, :, 0:HALF], ACT.Ln, bias=eps[:, 0:1], scale=1.0 / D
                                     ).then_inc(ln_done, 1)
                act.wait_ge(ln_done, val(i + 1))
                nc.scalar.activation(rs[:], rs[:], ACT.Exp, scale=-0.5).then_inc(r_ready, 1)

            def swap(g, n, which):
                act.wait_ge(ps_read, val(n + 1))
                if some(g * 2 + which):
                    act.wait_ge(rope_done, val(g * 2 + which))
                src = proj(n.c % 2)
                for q in range(4):
                    o = q ^ 1
                    mv = nc.scalar.activation(halves(qsw[32 * q:32 * q + 32, :]), src[32 * o:32 * o + 32], ACT.Copy)
                mv.then_inc(ps_swapped, 1)

            def k_hi(L, g, par):
                act.wait_ge(kpast_loaded, val((g + (G * L + 1)) * 16))
                act.wait_ge(pads_zero, val(6 * (L + 1)))
                if some((g + (G * L - 1)) * 10):
                    act.wait_ge(s_done, val((g + (G * L - 1)) * 10))
                if L == DIFF:
                    act.wait_ge(rope_done, val(g * 2 + 1))
                else:
                    act.wait_ge(ps_read, val(g * 3 + (N_LAYER * L + 1)))
                nc.scalar.activation(kh[par][:], kf[:], ACT.Copy).then_inc(kh_done, 1)

            def q_hi(L, g, par):
                if L == DIFF:
                    act.wait_ge(rope_done, val(g * 2 + 2))
                else:
                    act.wait_ge(ps_read, val(g * 3 + (N_LAYER * L + 2)))
                if some((g + (G * L - 1)) * 10):
                    act.wait_ge(s_done, val((g + (G * L - 1)) * 10))
                nc.scalar.activation(qh[par][:, 0:T], qf[:], ACT.Copy, scale=QK_SCALE).then_inc(qh_done, 1)

            def take_v(L, a):
                gi = a + G * L
                act.wait_ge(vt_done, val(gi + 1))
                if some(gi):
                    act.wait_ge(vl_done, val(gi))
                if some(gi):
                    act.wait_ge(vh_done, val(gi))
                nc.scalar.activation(vr[:, 0:4, :], tps[:], ACT.Copy).then_inc(vr_done, 1)
                nc.scalar.activation(vr[:, 4, :], ops[:, 0:P], ACT.Copy).then_inc(vr_done, 1)
                act.wait_ge(vr_done, val((gi + 1) * 2))
                act.wait_ge(vpast_loaded, val((gi + 1) * 16))
                if some(v_index(L, a, 0)):
                    act.wait_ge(pvp_done, val(v_index(L, a, 0)))
                nc.scalar.activation(vh[:], vr[:], ACT.Copy).then_inc(vh_done, 1)

            def exps(L, a, par, jj):
                i, h = JOBS[L][jj]
                J = (a + G * L) * 10 + jj
                slot = (10 * par + jj) % 4
                act.wait_ge(max_done, val(J + 1))
                if L == DIFF:
                    if some(a * 5 + ((jj - 4) // 2 + 1)):
                        act.wait_ge(t_done, val(a * 5 + ((jj - 4) // 2 + 1)))
                elif later(a) or jj >= 4:
                    act.wait_ge(t_done, val(a * 10 + (5 * G + jj - 3)))
                nc.scalar.activation(pr[:, slot, 0:width(i)], sps[:, jj % 2, 0:width(i)], ACT.Exp,
                                     bias=nmax[:, slot:slot + 1], accum_out=den[:, slot:slot + 1]
                                     ).then_inc(exp_done, 1)

            def take_p(L, a, tt):
                i, h = JOBS[L][2 * tt if L == DIFF else tt]
                tau = t_index(L, a, tt)
                act.wait_ge(t_done, val(tau + 1))
                if i == 4:
                    if some(v_index(L, a, h if L == FOX else 0)):
                        act.wait_ge(pvs_done, val(v_index(L, a, h if L == FOX else 0)))
                    dst, src = psh[:], tps[:, 0:3, :]
                else:
                    if some(v_index(L, a, h if L == FOX else 0)):
                        act.wait_ge(pvp_done, val(v_index(L, a, h if L == FOX else 0)))
                    dst, src = pth[:, 0:i + 1, P * i:P * i + P], tps[:, 0:i + 1, :]
                nc.scalar.activation(dst, src, ACT.Copy).then_inc(pt_hi, 1)

            def take_o(L, a, h, prompt):
                cols, src, done, taken = ((slice(0, SEQ), slice(0, SEQ), pvp_done, op_hi) if prompt else
                                          (slice(SEQ, T), slice(0, NEW), pvs_done, os_hi))
                act.wait_ge(done, val(v_index(L, a, h) + 1))
                if L == DIFF:
                    if some(a):
                        act.wait_ge(ol_done, val(a))
                    nc.scalar.activation(og[:, cols], ops[:, src], ACT.Copy).then_inc(taken, 1)
                else:
                    r = slice(64 * h, 64 * h + 64)
                    act.wait_ge(lf_stored, 16)
                    nc.scalar.activation(at_cols(oh, a, r, cols), ops[r, src], ACT.Copy).then_inc(taken, 1)

            def head_scale(a):
                act.wait_ge(oss_done, val(a + 1))
                act.wait_ge(on_done, val(a + 1))
                nc.scalar.activation(ors[:, 0:SEQ], ops[:], ACT.Ln, bias=eps[:, 1:2], scale=1.0 / P)
                nc.scalar.activation(ors[:, SEQ:T], tps[:, 0, 0:NEW], ACT.Ln, bias=eps[:, 1:2], scale=1.0 / P
                                     ).then_inc(oln_done, 1)
                act.wait_ge(oln_done, val(a + 1))
                nc.scalar.activation(ors[:], ors[:], ACT.Exp, scale=-0.5).then_inc(ors_done, 1)

            def o_hi(a):
                act.wait_ge(on_done, val(a + 2))
                apart()
                nc.scalar.activation(at(oh, a), og[:], ACT.Copy).then_inc(oh_done, 1)

            def attention(L, a, par, slot, first=False):
                if slot == VT_AT + 1:
                    take_v(L, a)
                if L == DIFF and not first:
                    if slot == SS_AT + 1:
                        head_scale(a - 1)
                    if slot == SS_AT + 3:
                        o_hi(a - 1)
                for jj in range(10):
                    if S_AT[L][jj] == slot:
                        exps(L, a, par, jj)
                for tt in range(len(T_AT[L])):
                    if T_AT[L][tt] == slot:
                        take_p(L, a, tt)
                for h in range(len(PVS_AT[L])):
                    if PVS_AT[L][h] == slot:
                        take_o(L, a, h, False)
                    if PVP_AT[L][h] == slot:
                        take_o(L, a, h, True)

            def group(L, g, par, first=False, alone=False):
                u, n = g * 3 + U_LAYER * L, g * 3 + N_LAYER * L
                for slot in range(SLOTS):
                    if not alone:
                        attention(L, g - 1, 1 - par, slot, first)
                    if alone and L == FOX and slot == 0:
                        act.wait_ge(f_loaded, 16)
                        nc.scalar.activation(f_hi[:], f_raw[:], ACT.Copy).then_inc(f_hi_done, 1)
                        scale_of_norm(2)
                    if alone and L == DIFF and slot == 0:
                        scale_of_norm(0)
                    if alone and L == FOX and slot == 13:
                        forget()
                    if slot == 8:
                        lead(u + 1)
                        if L == DIFF:
                            swap(g, n, 0)
                    if slot == 12:
                        k_hi(L, g, par)
                    if slot == 16:
                        lead(u + 2)
                        if L == DIFF:
                            swap(g, n + 1, 1)
                    if slot == 20:
                        q_hi(L, g, par)
                lead(u + 3)

            def forget():
                act.wait_ge(f_step, 4)
                nc.scalar.activation(fe[:], fe[:], ACT.Exp, scale=-1.0).then_inc(f_exp, 1)
                act.wait_ge(f_exp, 1)
                nc.scalar.activation(fe[:], fe[:], ACT.Ln, bias=ones[:, 0:1]).then_inc(f_ln, 1)
                act.wait_ge(f_tr, 1)
                nc.scalar.activation(lft[:, 0:4, :], tps[:], ACT.Copy).then_inc(f_lt, 1)
                nc.scalar.activation(lft[:, 4, :], ops[:, 0:P], ACT.Copy).then_inc(f_lt, 1)
                act.wait_ge(f_step, 8)
                nc.scalar.activation(cumh[:], cum[:], ACT.Copy).then_inc(cum_hi, 1)

            act.wait_ge(eps_set, 2)
            act.wait_ge(cst_loaded, 48)
            split(Num(0))
            for k in range(KT):
                act.wait_ge(x_loaded[k], 16)
                prep(0, Num(k))
            act.wait_ge(lam_step, 2)
            nc.scalar.activation(nlam[:, 2:4], nlam[:, 0:2], ACT.Exp).then_inc(lam_exp, 1)
            lead(Num(0))
            for L in (DIFF, FOX):
                group(L, Num(0), 0, alone=True)
                group(L, Num(1), 1, first=True)
                with act.Fori(0, 3) as it:
                    for par in range(2):
                        group(L, Num(2 + par, 2, it), par)
                for slot in range(SLOTS):
                    attention(L, Num(7), 1, slot)
                if L == DIFF:
                    head_scale(Num(7))
                    o_hi(Num(7))
                with act.Fori(0, KT // 2) as it:
                    for s in range(2):
                        lead(Num(U_LAYER * L + U_WO + s + 1, 2, it))
                        act.wait_ge(ps_read, val(Num(N_LAYER * L + N_WO + s + 1, 2, it)))
                        prep(2 * L + 1, Num(s, 2, it))
                scale_of_norm(2 * L + 1)
                def gate_up(jt):
                    j = jt + FT * L
                    u, n = jt * 2 + (U_LAYER * L + U_IN), jt * 2 + (N_LAYER * L + N_IN)
                    lead(u + 1)
                    act.wait_ge(ps_read, val(n + 1))
                    if some(j):
                        act.wait_ge(hf_done, val(j))
                    nc.scalar.activation(sg[:], gf[:], ACT.Silu).then_inc(sg_done, 1)
                    lead(u + 2)
                    act.wait_ge(hf_done, val(j + 1))
                    apart()
                    nc.scalar.activation(at(hh, jt), hf[:], ACT.Copy).then_inc(hh_done, 1)

                gate_up(Num(0))
                with act.Fori(0, FT - 1) as it:
                    gate_up(Num(1, 1, it))

                def out_tile(n, u, last):
                    lead(u + 1, OUT_PARTS[2])
                    if not last:
                        lead(u + 2)
                        lead(u + 3)
                    act.wait_ge(ps_read, val(n + (N_LAYER * L + N_OUT + 1)))
                    prep(2 * L + 2, n)

                u = U_LAYER * L + U_OUT
                with act.Fori(0, KT // 2 - 1) as it:
                    for s in range(2):
                        out_tile(Num(s, 2, it), Num(u + 3 * s, 6, it), False)
                for n in range(KT - 2, KT):
                    out_tile(Num(n), Num(u + 3 * n), L == FOX and n == KT - 1)
            scale_of_norm(4)

        @block.gpsimd
        def _(pool):
            def lead(u, kts=KT):
                u = u + 1
                slot = u.c % 2
                pool.wait_ge(w_hi_done, val(u + 1))
                if some(u - 1):
                    pool.wait_ge(w_used, val(u - 1))
                nc.gpsimd.tensor_tensor(w_lo[slot][:, 0:kts, :], w_raw[slot][:, 0:kts, :],
                                        w_hi[slot][:, 0:kts, :].bitcast(F32), ALU.subtract).then_inc(w_lo_done, 1)

            def times_sin(g, which):
                pool.wait_ge(ps_swapped, val(g * 2 + (which + 1)))
                nc.gpsimd.tensor_tensor(qsw[:], qsw[:], sinr[:], ALU.mult).then_inc(part_done, 1)

            def v_lo(L, a):
                pool.wait_ge(vh_done, val(a + (G * L + 1)))
                nc.gpsimd.tensor_tensor(vl[:], vr[:], vh[:].bitcast(F32), ALU.subtract).then_inc(vl_done, 1)

            def o_square(a):
                pool.wait_ge(op_hi, val(a + 1))
                if some(a):
                    pool.wait_ge(oss_done, val(a))
                nc.gpsimd.tensor_tensor(osq[:], og[:], og[:], ALU.mult).then_inc(osq_done, 1)

            def group(L, g, alone=False):
                u = g * 3 + U_LAYER * L
                if alone and L == FOX:
                    pool.wait_ge(f_hi_done, 1)
                    nc.gpsimd.tensor_tensor(f_lo[:], f_raw[:], f_hi[:].bitcast(F32), ALU.subtract
                                            ).then_inc(f_lo_done, 1)
                if not alone:
                    v_lo(L, g - 1)
                lead(u + 1)
                if L == DIFF:
                    if alone:
                        pool.wait_ge(rope_scaled, 2)
                    times_sin(g, 0)
                lead(u + 2)
                if L == DIFF:
                    times_sin(g, 1)
                if L == DIFF and not alone:
                    o_square(g - 1)
                lead(u + 3)

            lead(Num(-1))
            lead(Num(0))
            for L in (DIFF, FOX):
                group(L, Num(0), alone=True)
                group(L, Num(1))
                with pool.Fori(0, 3) as it:
                    for par in range(2):
                        group(L, Num(2 + par, 2, it))
                v_lo(L, Num(7))
                if L == DIFF:
                    o_square(Num(7))
                with pool.Fori(0, KT // 2) as it:
                    for s in range(2):
                        lead(Num(U_LAYER * L + U_WO + s + 1, 2, it))
                def gate_up(jt):
                    j = jt + FT * L
                    u, n = jt * 2 + (U_LAYER * L + U_IN), jt * 2 + (N_LAYER * L + N_IN)
                    lead(u + 1)
                    lead(u + 2)
                    pool.wait_ge(sg_done, val(j + 1))
                    pool.wait_ge(ps_read, val(n + 2))
                    if some(j):
                        pool.wait_ge(hl_done, val(j))
                    nc.gpsimd.tensor_tensor(hf[:], sg[:], uf[:], ALU.mult).then_inc(hf_done, 1)

                gate_up(Num(0))
                with pool.Fori(0, FT - 1) as it:
                    gate_up(Num(1, 1, it))
                u = U_LAYER * L + U_OUT
                with pool.Fori(0, KT // 2 - 1) as it:
                    for s in range(2):
                        ut = Num(u + 3 * s, 6, it)
                        lead(ut + 1, OUT_PARTS[2])
                        lead(ut + 2)
                        lead(ut + 3)
                for n in range(KT - 2, KT):
                    lead(Num(u + 3 * n + 1), OUT_PARTS[2])
                    if L == DIFF or n < KT - 1:
                        lead(Num(u + 3 * n + 2))
                        lead(Num(u + 3 * n + 3))

        @block.vector
        def _(dve):
            tt = nc.vector.tensor_tensor
            stt = nc.vector.scalar_tensor_tensor

            def column(tile, n):
                if n.it is None or n.k == 0:
                    return tile[:, n.c:n.c + 1]
                return tile[:, bass.ds(n.v(), 1)]

            def prep(i, n):
                if i < 4:
                    dve.wait_ge(xh_done, val(n + (KT * i + 1)))
                    stt(at(xl, n), at(xT, n), column(norm_w[i], n), at(xh, n).bitcast(F32), ALU.mult, ALU.subtract
                        ).then_inc(xl_done, 1)
                dve.wait_ge(sq_done, val(n + (KT * i + 1)))
                if some(n + KT * i):
                    dve.wait_ge(acc_done, val(n + KT * i))
                tt(acc[:], acc[:], sqt[:], ALU.add).then_inc(acc_done, 1)

            def clear_acc(i):
                if some(i):
                    dve.wait_ge(ss_done, val(i))
                nc.vector.memset(acc[:], 0.0).then_inc(acc_zero, 1)
                dve.wait_ge(acc_zero, val(i + 1))

            def residual(units, n, k):
                dve.wait_ge(w_used, val(units))
                tt(halves(at(xT, k)), proj(n.c % 2), halves(at(xT, k)), ALU.add).then_inc(ps_read, 1)
                dve.wait_ge(ps_read, val(n + 1))

            def take(dst, units, n, scale):
                dve.wait_ge(w_used, val(units))
                tt(halves(dst), proj(n.c % 2), halves(scale), ALU.mult).then_inc(ps_read, 1)

            def take_k(L, g):
                gi = g + G * L
                if some(gi * 16):
                    dve.wait_ge(k_stored, val(gi * 16))
                if some(gi):
                    dve.wait_ge(kh_done, val(gi))
                take(kf[:, 0:T], g * 3 + (U_LAYER * L + 1), g * 3 + N_LAYER * L, (cosr if L == DIFF else rs)[:])

            def take_q(L, g):
                if some(g + G * L):
                    dve.wait_ge(qh_done, val(g + G * L))
                take(qf[:], g * 3 + (U_LAYER * L + 2), g * 3 + (N_LAYER * L + 1), (cosr if L == DIFF else rs)[:])

            def take_v(L, g):
                gi = g + G * L
                if some(gi):
                    dve.wait_ge(vt_done, val(gi))
                if some(gi * 16):
                    dve.wait_ge(v_stored, val(gi * 16))
                take(vf[:, 0:T], g * 3 + (U_LAYER * L + 3), g * 3 + (N_LAYER * L + 2), rs[:])

            def rotate(g, which):
                x = (kf, qf)[which]
                dve.wait_ge(part_done, val(g * 2 + (which + 1)))
                dve.wait_ge(ps_read, val(g * 3 + (which + 1)))
                tt(x[:, 0:T], x[:, 0:T], qsw[:], ALU.add).then_inc(rope_done, 1)

            def k_lo(L, g, par):
                dve.wait_ge(kh_done, val(g + (G * L + 1)))
                tt(kl[par][:], kf[:], kh[par][:].bitcast(F32), ALU.subtract).then_inc(kl_done, 1)

            def q_lo(L, g, par):
                dve.wait_ge(qh_done, val(g + (G * L + 1)))
                stt(ql[par][:, 0:T], qf[:], QK_SCALE, qh[par][:, 0:T].bitcast(F32), ALU.mult, ALU.subtract
                    ).then_inc(ql_done, 1)

            def row_max(L, a, par, jj):
                i, h = JOBS[L][jj]
                J = (a + G * L) * 10 + jj
                slot = (10 * par + jj) % 4
                dve.wait_ge(s_done, val(J + 1))
                nc.vector.tensor_reduce(nmax[:, slot:slot + 1], sps[:, jj % 2, 0:width(i)], AX_X, ALU.max,
                                        negate=True).then_inc(max_done, 1)

            def weigh(L, a, par, jj):
                i, h = JOBS[L][jj]
                w = width(i)
                tau = t_index(L, a, jj // 2 if L == DIFF else jj)
                dve.wait_ge(exp_done, val((a + G * L) * 10 + (jj + 1)))
                if L == DIFF:
                    sa = (10 * par + jj - 1) % 4
                    s_b = sa + 1
                    nc.vector.reciprocal(rden[:, sa:sa + 2], den[:, sa:sa + 2]).then_inc(rden_done, 1)
                    dve.wait_ge(rden_done, val(tau + 1))
                    tt(nlr[:, s_b:s_b + 1], rden[:, s_b:s_b + 1], nlam[:, 5:6], ALU.mult).then_inc(nlr_done, 1)
                    nc.vector.tensor_scalar(pr[:, sa, 0:w], pr[:, sa, 0:w], rden[:, sa:sa + 1], None, ALU.mult
                                            ).then_inc(pa_done, 1)
                    dve.wait_ge(nlr_done, val(tau + 1))
                    dve.wait_ge(pa_done, val(tau + 1))
                    stt(pr[:, sa, 0:w], pr[:, s_b, 0:w], nlr[:, s_b:s_b + 1], pr[:, sa, 0:w], ALU.mult, ALU.add
                        ).then_inc(p_ready, 1)
                else:
                    s = (10 * par + jj) % 4
                    nc.vector.reciprocal(rden[:, s:s + 1], den[:, s:s + 1]).then_inc(rden_done, 1)
                    dve.wait_ge(rden_done, val(tau + 1))
                    nc.vector.tensor_scalar(pr[:, s, 0:w], pr[:, s, 0:w], rden[:, s:s + 1], None, ALU.mult
                                            ).then_inc(p_ready, 1)

            def p_lo(L, a, tt_):
                i, h = JOBS[L][2 * tt_ if L == DIFF else tt_]
                dve.wait_ge(pt_hi, val(t_index(L, a, tt_) + 1))
                if i == 4:
                    dst, hi, src = psl[:], psh[:], tps[:, 0:3, :]
                else:
                    cols = slice(P * i, P * i + P)
                    dst, hi, src = ptl[:, 0:i + 1, cols], pth[:, 0:i + 1, cols], tps[:, 0:i + 1, :]
                tt(dst, src, hi.bitcast(F32), ALU.subtract).then_inc(pt_lo, 1)

            def o_lo(a, h, prompt):
                cols, src, done, taken = ((slice(0, SEQ), slice(0, SEQ), op_hi, op_lo) if prompt else
                                          (slice(SEQ, T), slice(0, NEW), os_hi, os_lo))
                r = slice(64 * h, 64 * h + 64)
                dve.wait_ge(done, val(v_index(FOX, a, h) + 1))
                tt(at_cols(ol, a, r, cols), ops[r, src], at_cols(oh, a, r, cols).bitcast(F32), ALU.subtract
                   ).then_inc(taken, 1)

            def norm_o(a):
                dve.wait_ge(ors_done, val(a + 1))
                stt(og[:], og[:], sub_w[:], ors[:], ALU.mult, ALU.mult).then_inc(on_done, 1)

            def split_o(a):
                dve.wait_ge(oh_done, val(a + 1))
                tt(at(ol, a), og[:], at(oh, a).bitcast(F32), ALU.subtract).then_inc(ol_done, 1)

            def aug_left(g):
                for h in range(2):
                    if later(g):
                        dve.wait_ge(s_done, val((g + (G - 1)) * 10 + 5 * (h + 1)))
                    nc.vector.tensor_scalar(aug_l[h][:], aug_m[:], column(head_sel, g * 2 + h), None, ALU.mult
                                            ).then_inc(aug_l_done, 1)

            def attention(L, a, par, slot, first=False):
                if L == DIFF and not first:
                    if slot == SS_AT + 2:
                        norm_o(a - 1)
                    if slot == SS_AT + 4:
                        split_o(a - 1)
                for jj in range(10):
                    if S_AT[L][jj] == slot:
                        row_max(L, a, par, jj)
                for jj in range(10):
                    if S_AT[L][jj] + 1 == slot and (L == FOX or jj % 2):
                        weigh(L, a, par, jj)
                for t in range(len(T_AT[L])):
                    if T_AT[L][t] == slot:
                        p_lo(L, a, t)
                if L == FOX:
                    for h in range(2):
                        if PVS_AT[L][h] == slot:
                            o_lo(a, h, False)
                        if PVP_AT[L][h] == slot:
                            o_lo(a, h, True)

            def group(L, g, par, first=False, alone=False):
                for slot in range(SLOTS):
                    if not alone:
                        attention(L, g - 1, 1 - par, slot, first)
                    if slot == 8:
                        take_k(L, g)
                    if slot == 9 and alone and L == FOX:
                        forget_1()
                    if slot == 11 and L == DIFF:
                        rotate(g, 0)
                    if slot == 12:
                        k_lo(L, g, par)
                    if slot == 16:
                        take_q(L, g)
                    if slot == 17 and alone and L == FOX:
                        forget_2()
                    if slot == 19 and L == DIFF:
                        rotate(g, 1)
                    if slot == 20:
                        q_lo(L, g, par)
                        if L == FOX:
                            aug_left(g)
                take_v(L, g)

            def forget_1():
                nc.vector.memset(lf[:, T:TQ], 0.0).then_inc(f_step, 1)
                dve.wait_ge(f_proj, 1)
                tt(halves(fz[:]), sps[:, :, 0:HALF], halves(rs[:]), ALU.mult).then_inc(f_step, 1)
                dve.wait_ge(f_step, 2)
                nc.vector.tensor_scalar(fz[:], fz[:], b_f, None, ALU.add).then_inc(f_step, 1)
                dve.wait_ge(f_step, 3)
                stt(fe[:], fz[:], -1.0, fz[:], ALU.mult, ALU.max).then_inc(f_step, 1)
                dve.wait_ge(f_ln, 1)
                stt(lf[:, 0:T], fz[:], 0.0, fe[:], ALU.min, ALU.subtract).then_inc(f_step, 1)

            def forget_2():
                dve.wait_ge(f_cum, 1)
                nc.vector.tensor_copy(cum[:, 0:SEQ], sps[:, 0, :]).then_inc(f_step, 1)
                nc.vector.tensor_copy(cum[:, TQ:TK], sps[:, 1, 0:PAST]).then_inc(f_step, 1)
                nc.vector.tensor_copy(cum[:, SEQ:TQ], sps[:, 1, PAST:PAST + P]).then_inc(f_step, 1)
                dve.wait_ge(cum_hi, 1)
                nc.vector.memset(aug_m[0:64, :], 1.0).then_inc(f_step, 1)
                nc.vector.tensor_copy(aug_m[64:96, :], cumh[64:96, 0:TQ].bitcast(F32)).then_inc(f_step, 1)
                tt(aug_m[96:128, :], cum[96:128, 0:TQ], cumh[96:128, 0:TQ].bitcast(F32), ALU.subtract
                   ).then_inc(f_step, 1)
                nc.vector.tensor_scalar(aug_r[0:32, :], cumh[0:32, :].bitcast(F32), -1.0, None, ALU.mult
                                        ).then_inc(f_step, 1)
                tt(aug_r[32:64, :], cumh[32:64, :].bitcast(F32), cum[32:64, :], ALU.subtract).then_inc(f_step, 1)
                nc.vector.memset(aug_r[64:128, :].bitcast(F32), 1.0).then_inc(f_step, 1)
                dve.wait_ge(f_step, 14)

            def clear_pads():
                for s in range(2):
                    nc.vector.memset(qh[s][:, T:TQ].bitcast(F32), 0.0).then_inc(pads_zero, 1)
                    nc.vector.memset(ql[s][:, T:TQ].bitcast(F32), 0.0).then_inc(pads_zero, 1)
                nc.vector.memset(kf[:, T:TQ], 0.0).then_inc(pads_zero, 1)
                nc.vector.memset(vf[:, T:TQ], 0.0).then_inc(pads_zero, 1)

            nc.vector.memset(eps[:, 0:1], EPS).then_inc(eps_set, 1)
            nc.vector.memset(eps[:, 1:2], SUB_EPS).then_inc(eps_set, 1)
            clear_pads()
            clear_acc(0)
            dve.wait_ge(cst_loaded, 48)
            for k in range(KT):
                prep(0, Num(k))
            tt(og[:, 0:P], lam_p[:, 0:P], lam_p[:, P:2 * P], ALU.mult).then_inc(lam_step, 1)
            dve.wait_ge(lam_step, 1)
            nc.vector.tensor_reduce(nlam[:, 0:2], og[:, 0:P].rearrange("p (a b) -> p a b", a=2), AX_X, ALU.add
                                    ).then_inc(lam_step, 1)
            dve.wait_ge(lam_exp, 1)
            tt(nlam[:, 4:5], nlam[:, 3:4], nlam[:, 2:3], ALU.subtract).then_inc(lam_step, 1)
            dve.wait_ge(lam_step, 3)
            nc.vector.tensor_scalar(nlam[:, 5:6], nlam[:, 4:5], -LAM_INIT, None, ALU.add).then_inc(lam_step, 1)
            nc.vector.tensor_scalar(sub_w[:], subln, 1.0 - LAM_INIT, None, ALU.mult).then_inc(on_done, 1)
            dve.wait_ge(rope_loaded, 32)
            dve.wait_ge(r_ready, 1)
            dve.wait_ge(lam_step, 4)
            dve.wait_ge(on_done, 1)
            tt(cosr[:], cosr[:], rs[:], ALU.mult).then_inc(rope_scaled, 1)
            tt(sinr[:], sinr[:], rs[:], ALU.mult).then_inc(rope_scaled, 1)
            dve.wait_ge(rope_scaled, 2)
            for L in (DIFF, FOX):
                if L == FOX:
                    clear_pads()
                    dve.wait_ge(r_ready, 3)
                group(L, Num(0), 0, alone=True)
                group(L, Num(1), 1, first=True)
                with dve.Fori(0, 3) as it:
                    for par in range(2):
                        group(L, Num(2 + par, 2, it), par)
                for slot in range(SLOTS):
                    attention(L, Num(7), 1, slot)
                if L == DIFF:
                    norm_o(Num(7))
                    split_o(Num(7))
                clear_acc(2 * L + 1)
                with dve.Fori(0, KT // 2) as it:
                    for s in range(2):
                        k = Num(s, 2, it)
                        residual(k + (U_LAYER * L + U_WO + 1), k + (N_LAYER * L + N_WO), k)
                        prep(2 * L + 1, k)
                dve.wait_ge(r_ready, val(2 * L + 2))

                def gate_up(jt):
                    j = jt + FT * L
                    u, n = jt * 2 + (U_LAYER * L + U_IN), jt * 2 + (N_LAYER * L + N_IN)
                    if some(j):
                        dve.wait_ge(sg_done, val(j))
                    take(gf[:], u + 1, n, rs[:])
                    if some(j):
                        dve.wait_ge(hf_done, val(j))
                    take(uf[:], u + 2, n + 1, rs[:])
                    dve.wait_ge(hh_done, val(j + 1))
                    tt(at(hl, jt), hf[:], at(hh, jt).bitcast(F32), ALU.subtract).then_inc(hl_done, 1)

                gate_up(Num(0))
                with dve.Fori(0, FT - 1) as it:
                    gate_up(Num(1, 1, it))
                clear_acc(2 * L + 2)
                with dve.Fori(0, KT // 2) as it:
                    for s in range(2):
                        k = Num(s, 2, it)
                        residual(Num(U_LAYER * L + U_OUT + 3 * (s + 1), 6, it), k + (N_LAYER * L + N_OUT), k)
                        prep(2 * L + 2, k)
            dve.wait_ge(r_ready, 5)
            for k in range(KT):
                stt(yt[:, k, :], xT[:, k, :], norm_w[4][:, k:k + 1], rs[:], ALU.mult, ALU.mult).then_inc(y_done, 1)


def at_cols(tile, i, rows, cols):
    if i.it is None or i.k == 0:
        return tile[rows, i.c, cols]
    return tile[rows, bass.ds(i.v(), 1), cols].rearrange("p a b -> p (a b)")


def kernel(**inputs):
    import numpy as np
    import ml_dtypes
    import concourse.bacc as bacc
    from concourse.bass_utils import run_bass_kernel_spmd as run

    a = {k: np.asarray(v) for k, v in inputs.items()}

    def units(w):
        k, n = w.shape
        return w.reshape(k // P, P, n // P, P).transpose(2, 1, 0, 3).reshape(n // P, P, k)

    def pad(w, width_):
        out = np.zeros(w.shape[:-1] + (width_,), w.dtype)
        out[..., :w.shape[-1]] = w
        return out

    stream = []
    for L, (w_in, w_o) in enumerate(((a["diff_w_qkv"][0], a["diff_w_o"][0]), (a["fox_w_qkvf"][0], a["fox_w_o"][0]))):
        q, k, v = (units(w_in[:, i * D:(i + 1) * D]) for i in range(3))
        stream += [x for g in range(G) for x in (k[g:g + 1], q[g:g + 1], v[g:g + 1])]
        stream.append(units(w_o))
        gate, up = units(a["ffn_w_in"][L][:, :F]), units(a["ffn_w_in"][L][:, F:])
        stream.append(np.stack([gate, up], 1).reshape(2 * FT, P, D))
        out = units(a["ffn_w_out"][L])
        stream.append(pad(out, 3 * D).reshape(KT, P, 3, D).transpose(0, 2, 1, 3).reshape(3 * KT, P, D))
    w_units = np.concatenate(stream)

    def quadrants(x):
        out = np.zeros(x.shape[:-1] + (4, 32), x.dtype)
        out[..., :, :2 * G] = x[..., None, :]
        return out.reshape(x.shape[:-1] + (P,))

    w_forget = units(quadrants(a["fox_w_qkvf"][0][:, 3 * D:]))[0]
    x_in = np.concatenate([a["x_prompt"][0], a["x_sample"][0]]).T
    cols = [a[n][i].reshape(KT, P).T for i in range(2) for n in ("norm_mix", "norm_ffn")]
    lam = a["diff_lambda"][0]
    small = np.concatenate(
        cols + [a["norm_final"].reshape(KT, P).T, a["diff_subln"][0][:, None], quadrants(a["fox_b_f"][0])[:, None],
                np.broadcast_to(lam[[0, 2, 1, 3]].reshape(1, 2 * P), (P, 2 * P))], 1)
    tri = np.triu(np.ones((P, P), np.float32))
    sel = quadrants(np.eye(2 * G, dtype=np.float32)).T
    cst = np.concatenate([np.eye(P, dtype=np.float32), np.ones((P, P), np.float32), sel,
                          tri, np.ones((P, SEQ - P), np.float32)], 1)
    chunk = np.arange(P) // 64
    masked = np.float32(-1e30)
    cst16 = np.concatenate([np.eye(P), np.where(chunk[None] <= chunk[:, None], 0, masked),
                            np.where(np.arange(P)[None] <= np.arange(P)[:, None], 0, masked)], 1
                           ).astype(ml_dtypes.bfloat16)
    pos = np.concatenate([np.arange(SEQ), PAST + np.arange(NEW)]).astype(np.float32)
    freq = (10000.0 ** -(np.arange(32) / 32)).astype(np.float32)
    ang = freq[:, None] * pos[None]
    cos, sin = np.cos(ang), np.sin(ang)
    rope_tab = np.concatenate([np.tile(cos, (4, 1)), np.concatenate([-sin, sin, -sin, sin])], 1)
    k_past = np.concatenate([a["cache_diff_k"][0, 0].reshape(PAST, D).T, a["cache_fox_k"][0, 0].reshape(PAST, D).T])

    def frames(x):
        return x.reshape(2, P, -1, P).transpose(2, 1, 0, 3).reshape(-1, P, 2 * P)

    v_past = np.concatenate([frames(a["cache_diff_v"][0, 0].reshape(PAST, D)),
                             frames(a["cache_fox_v"][0, 0].reshape(PAST, D))])
    f_past = frames(quadrants(a["cache_fox_logf"][0, 0]))[0]

    nc = bacc.Bacc("TRN2", target_bir_lowering=False, num_devices=1)
    arrays, args = {}, []
    for name, x in (("w_units", w_units), ("w_forget", w_forget), ("x_in", x_in), ("small", small), ("cst", cst),
                    ("cst16", cst16), ("rope_tab", rope_tab), ("k_past", k_past), ("v_past", v_past),
                    ("f_past", f_past)):
        x = np.ascontiguousarray(x)
        arrays[name] = x
        args.append(nc.dram_tensor(name, x.shape, mybir.dt.from_np(x.dtype), kind="ExternalInput").ap())
    outs = (("y_out", D), ("dk_out", D), ("dv_out", D), ("fk_out", D), ("fv_out", D), ("lf_out", 2 * G))
    for name, rows in outs:
        args.append(nc.dram_tensor(name, (rows, T), F32, kind="ExternalOutput").ap())
    encoder(nc, *args)
    got = run(nc, [arrays], core_ids=[0]).results[0]
    y, dk, dv, fk, fv, lf = (np.ascontiguousarray(got[name].T) for name, _ in outs)

    def part(x, s, shape):
        x = x[:SEQ] if s == 0 else x[SEQ:]
        return x.reshape(shape[:2] + (x.shape[0],) + shape[2:])

    res = [y[:SEQ].reshape(1, SEQ, D), y[SEQ:].reshape(1, NEW, D)]
    for s in range(2):
        res += [part(dk, s, (1, 1, 16, 64)), part(dv, s, (1, 1, 8, 128)), part(fk, s, (1, 1, 16, 64)),
                part(fv, s, (1, 1, 16, 64)), part(lf, s, (1, 1, 16))]
    return tuple(res)
```

```python
from contextlib import ExitStack

import concourse.bass as bass
from concourse import mybir

F32 = mybir.dt.float32
F32R = mybir.dt.float32r
BF16 = mybir.dt.bfloat16
ALU = mybir.AluOpType
ACT = mybir.ActivationFunctionType
AX_X = mybir.AxisListType.X

P = 128
D = 1024
KT = D // P
SEQ, NEW, PAST = 512, 64, 256
T = SEQ + NEW
HALF = T // 2
TQ = SEQ + P
TK = SEQ + P + PAST
G = 8
F = 2816
FT = F // P
OUT_PARTS = (8, 8, 6)
U_WO, U_IN, U_OUT, U_LAYER = 24, 32, 76, 100
N_WO, N_IN, N_OUT, N_LAYER = 24, 36, 80, 88
WO_STEPS = ([(j, 2 + j, k) for j in (0, 1) for k in range(6)] + [(0, 2, 6), (1, 3, 6)]
            + [(j, 2 + j, k) for j in (2, 3) for k in range(7)]
            + [(4 + t, t, k) for t in (0, 1) for k in range(7)] + [(4 + t, t, 7) for t in range(6)]
            + [(4 + t, t, k) for t in (6, 7) for k in range(KT)])
WO_OPEN = [next(q for q, s in enumerate(WO_STEPS) if s[0] == j) for j in range(12)]
WO_END = [max(q for q, s in enumerate(WO_STEPS) if s[0] == j) for j in range(12)]
WO_EARLY = 9
SLOTS = 24
QK_SCALE = 0.125
EPS, SUB_EPS = 1e-6, 1e-5
LAM_INIT = 0.2
DIFF, FOX = 0, 1

LATE = -1
LAST_PV = 4
JOBS = {DIFF: [(i, h) for i in (4, 3, 2, 1, 0) for h in (0, 1)],
        FOX: [(i, h) for h in (0, 1) for i in (4, 3, 2, 1, 0)]}
S_AT = {DIFF: [0, 1, 3, 4, 7, 8, 11, 12, 15, 16], FOX: [0, 1, 3, 5, 8, 10, 12, 14, 16, 18]}
T_AT = {DIFF: [6, 9, 13, 17, 21], FOX: [4, 6, 8, 10, 12, 14, 17, 19, 21, 23]}
PVS_AT = {DIFF: [9], FOX: [9, 17]}
PVP_AT = {DIFF: [LATE], FOX: [14, LATE]}
VT_AT, SS_AT = 2, 4
SWAP_AT = (9, 16)
ROTATE_AT = (13, 21)
LEAD_AT = {DIFF: 18, FOX: 17}
K_HI_AT = {DIFF: 14, FOX: 12}
K_LO_AT = {DIFF: 17, FOX: 12}
TAKE_Q_AT = {DIFF: 16, FOX: 18}
Q_AT = {DIFF: 21, FOX: 20}
NORM0_AT = 3


class Num:

    def __init__(self, c, k=0, it=None):
        self.c, self.k, self.it = c, k, it

    def __add__(self, n):
        return Num(self.c + n, self.k, self.it)

    def __sub__(self, n):
        return self + (-n)

    def __mul__(self, n):
        return Num(self.c * n, self.k * n, self.it)

    def half(self):
        assert self.k % 2 == 0
        return Num(self.c // 2, self.k // 2, self.it)

    def v(self):
        return self.c if self.it is None or self.k == 0 else self.it * self.k + self.c


def val(n):
    n = n if isinstance(n, Num) else Num(n)
    assert n.c > 0, n.c
    return n.v()


def some(n):
    return n > 0 if isinstance(n, int) else n.c > 0 or n.it is not None


def later(g):
    return some(g)


def at(tile, i):
    if i.it is None or i.k == 0:
        return tile[:, i.c, :]
    return tile[:, bass.ds(i.v(), 1), :].rearrange("p a b -> p (a b)")


def width(i):
    return 3 * P if i == 4 else (i + 1) * P


def encoder(nc, w_units, w_forget, x_in, small, cst, cst16, rope_tab, k_past, v_past, f_past,
            y_out, dk_out, dv_out, fk_out, fv_out, lf_out):
    k_out = (dk_out, fk_out)
    v_out = (dv_out, fv_out)
    with ExitStack() as ctx:
        def sb(name, shape, dt=F32):
            return ctx.enter_context(nc.sbuf_tensor(name, shape, dt))

        def sem(name):
            return ctx.enter_context(nc.semaphore(name))

        xT = sb("xT", [P, KT, T])
        xh = sb("xh", [P, KT, T], F32R)
        xl = sb("xl", [P, KT, T], F32R)
        w_raw = [sb(f"w_raw{s}", [P, KT, P]) for s in range(2)]
        w_hi = [sb(f"w_hi{s}", [P, KT, P], F32R) for s in range(2)]
        w_lo = [sb(f"w_lo{s}", [P, KT, P], F32R) for s in range(2)]
        rs = sb("rs", [P, T])
        acc = sb("acc", [P, T])
        smalls = sb("smalls", [P, 5 * KT + 2 + 2 * P])
        norm_w = [smalls[:, KT * i:KT * (i + 1)] for i in range(5)]
        c0 = 5 * KT
        subln, b_f, lam_p = smalls[:, c0:c0 + 1], smalls[:, c0 + 1:c0 + 2], smalls[:, c0 + 2:c0 + 2 + 2 * P]
        cstf = sb("cstf", [P, 2 * P + 2 * G])
        ident, ones, head_sel = cstf[:, 0:P], cstf[:, P:2 * P], cstf[:, 2 * P:2 * P + 2 * G]
        csth = sb("csth", [P, 3 * P], BF16)
        ident16, mask = csth[:, 0:P], (csth[:, P:2 * P], csth[:, 2 * P:3 * P])
        eps = sb("eps", [P, 2])
        nlam = sb("nlam", [P, 8])
        sub_w = sb("sub_w", [P, 1])
        nmax = sb("nmax", [P, 4])
        den = sb("den", [P, 4])
        rden = sb("rden", [P, 4])
        nlr = sb("nlr", [P, 4])

        ARENA = 121344
        arena_start = -(-nc.sbuf_base // 32) * 32
        assert arena_start + ARENA <= nc.sbuf_usable_end
        holder = {"at": 0}

        def place(name, shape, dt=F32, offset=None):
            n = 4
            for s in shape[1:]:
                n *= s
            if offset is None:
                offset = holder["at"]
                holder["at"] += n
            assert offset + n <= ARENA, name
            return nc.alloc_sbuf_tensor_at(name, shape, dt, offset=arena_start + offset)

        qh = [place(f"qh{s}", [P, TQ], F32R) for s in range(2)]
        ql = [place(f"ql{s}", [P, TQ], F32R) for s in range(2)]
        kh = [place(f"kh{s}", [P, TK], F32R) for s in range(2)]
        kl = [place(f"kl{s}", [P, TK], F32R) for s in range(2)]
        qf = place("qf", [P, T])
        kf = place("kf", [P, TK])
        vf = place("vf", [P, TQ])
        vr = place("vr", [P, 7, P])
        vh = place("vh", [P, 7, P], F32R)
        vl = place("vl", [P, 7, P], F32R)
        pr = place("pr", [P, 4, SEQ])
        pt_at = holder["at"]
        pth = place("pth", [P, 4, SEQ], F32R)
        ptl = place("ptl", [P, 4, SEQ], F32R)
        pts = place("pts", [P, 3, 2 * NEW], F32R)
        os2 = place("os2", [P, 2 * NEW])
        osum = place("osum", [P, NEW])
        o_at = holder["at"]
        oh = place("oh", [P, G, T], F32R)
        ol = place("ol", [P, G, T], F32R)
        own_at = holder["at"]
        cosr = place("cosr", [P, T])
        sinr = place("sinr", [P, T])
        qsw = place("qsw", [P, T])
        og = place("og", [P, T])
        osq = place("osq", [P, T])
        ors = place("ors", [P, T])
        holder["at"] = own_at
        aug_m = place("aug_m", [P, TQ])
        aug_r = place("aug_r", [P, TK], F32R)
        aug_l = [place(f"aug_l{h}", [P, TQ], F32R) for h in range(2)]
        holder["at"] = pt_at
        f_raw = place("f_raw", [P, KT, P])
        f_hi = place("f_hi", [P, KT, P], F32R)
        f_lo = place("f_lo", [P, KT, P], F32R)
        holder["at"] = o_at
        fz = place("fz", [P, T])
        fe = place("fe", [P, T])
        lf = place("lf", [P, TQ])
        lft = place("lft", [P, 7, P])
        cum = place("cum", [P, TK])
        cumh = place("cumh", [P, TK], F32R)
        upper = place("upper", [P, SEQ])
        holder["at"] = 0
        hh = place("hh", [P, FT, T], F32R)
        hl = place("hl", [P, FT, T], F32R)
        gf = place("gf", [P, T])
        sg = place("sg", [P, T])
        uf = place("uf", [P, T])
        hf = place("hf", [P, T])
        sqt = place("sqt", [P, T], offset=ARENA - 4 * T)
        sq_all = place("sq_all", [P, KT, T], offset=o_at)
        yt = place("yt", [P, KT, T], offset=0)

        ps = ctx.enter_context(nc.psum_tensor("ps", [P, 4, 512], F32))
        sps = ctx.enter_context(nc.psum_tensor("sps", [P, 2, 512], F32))
        tps = ctx.enter_context(nc.psum_tensor("tps", [P, 4, P], F32))
        ops = ctx.enter_context(nc.psum_tensor("ops", [P, 512], F32))

        def proj(n2):
            return ps[:, 2 * n2:2 * n2 + 2, 0:HALF]

        def halves(ap):
            return ap.rearrange("p (a b) -> p a b", a=2)

        x_loaded = [sem(f"x_loaded{k}") for k in range(KT)]
        small_loaded = sem("small_loaded")
        cst_loaded = sem("cst_loaded")
        rope_loaded = sem("rope_loaded")
        w_loaded = [sem(f"w_loaded{s}") for s in range(2)]
        f_loaded = sem("f_loaded")
        upper_loaded = sem("upper_loaded")
        fpast_loaded = sem("fpast_loaded")
        kpast_loaded = sem("kpast_loaded")
        vpast_loaded = sem("vpast_loaded")
        k_stored = sem("k_stored")
        v_stored = sem("v_stored")
        lf_stored = sem("lf_stored")
        y_stored = sem("y_stored")
        w_hi_done = sem("w_hi_done")
        w_lo_done = sem("w_lo_done")
        w_lo_first = sem("w_lo_first")
        w_used = sem("w_used")
        wo_done = sem("wo_done")
        ps_read = sem("ps_read")
        ps_swapped = sem("ps_swapped")
        xh_done = sem("xh_done")
        xl_done = sem("xl_done")
        sq_done = sem("sq_done")
        sq_act = sem("sq_act")
        sq_pool = sem("sq_pool")
        acc_done = sem("acc_done")
        acc_zero = sem("acc_zero")
        ss_done = sem("ss_done")
        ln_done = sem("ln_done")
        r_ready = sem("r_ready")
        pads_zero = sem("pads_zero")
        eps_set = sem("eps_set")
        lam_step = sem("lam_step")
        lam_exp = sem("lam_exp")
        rope_scaled = sem("rope_scaled")
        part_done = sem("part_done")
        rope_done = sem("rope_done")
        kh_done = sem("kh_done")
        kl_done = sem("kl_done")
        qh_done = sem("qh_done")
        ql_done = sem("ql_done")
        vt_done = sem("vt_done")
        vr_done = sem("vr_done")
        vh_done = sem("vh_done")
        vl_done = sem("vl_done")
        s_done = sem("s_done")
        max_done = sem("max_done")
        exp_done = sem("exp_done")
        rden_done = sem("rden_done")
        nlr_done = sem("nlr_done")
        pa_done = sem("pa_done")
        p_ready = sem("p_ready")
        t_done = sem("t_done")
        pt_hi = sem("pt_hi")
        pt_lo = sem("pt_lo")
        pvs_done = sem("pvs_done")
        pvp_done = sem("pvp_done")
        os_taken = sem("os_taken")
        os_summed = sem("os_summed")
        os_hi = sem("os_hi")
        op_hi = sem("op_hi")
        op_lo = sem("op_lo")
        osq_done = sem("osq_done")
        oss_done = sem("oss_done")
        oln_done = sem("oln_done")
        ors_done = sem("ors_done")
        on_done = sem("on_done")
        oh_done = sem("oh_done")
        ol_done = sem("ol_done")
        aug_l_done = sem("aug_l_done")
        f_hi_done = sem("f_hi_done")
        f_lo_done = sem("f_lo_done")
        f_proj = sem("f_proj")
        f_step = sem("f_step")
        aug_ones = sem("aug_ones")
        f_exp = sem("f_exp")
        f_ln = sem("f_ln")
        f_tr = sem("f_tr")
        f_lt = sem("f_lt")
        f_cum = sem("f_cum")
        cum_hi = sem("cum_hi")
        sg_done = sem("sg_done")
        hf_done = sem("hf_done")
        hh_done = sem("hh_done")
        hl_done = sem("hl_done")
        y_done = sem("y_done")

        def t_index(L, a, jj):
            return a * 5 + jj if L == DIFF else a * 10 + (5 * G + jj)

        def v_index(L, a, h):
            return a if L == DIFF else a * 2 + (G + h)

        def prep_count(L, ffn, k):
            return KT * (2 * L + ffn) + k

        block = ctx.enter_context(nc.Block())

        @block.sync
        def _(sp):
            def load_unit(u, cols=KT):
                slot = u.c % 2
                if u.it is None and u.c == 2:
                    sp.wait_ge(w_lo_first, 1)
                if some(u - 1):
                    sp.wait_ge(w_hi_done, val(u - 1))
                if some(u - 1):
                    sp.wait_ge(w_lo_done, val(u - 1))
                if u.it is None or u.k == 0:
                    src = w_units[u.c]
                else:
                    src = w_units[bass.ds(u.v(), 1)].rearrange("a p n -> (a p) n")
                sp.dma_start(w_raw[slot][:, 0:cols, :], src[:, 0:cols * P].rearrange("p (k n) -> p k n", n=P)
                             ).then_inc(w_loaded[slot], 16)

            def rows(dram, g):
                if g.it is None or g.k == 0:
                    return dram[P * g.c:P * (g.c + 1), :]
                return dram[bass.ds((g * P).v(), P), :]

            def store_v(L, g):
                sp.wait_ge(ps_read, val(g * 3 + (N_LAYER * L + 3)))
                sp.dma_start(rows(v_out[L], g), vf[:, 0:T]).then_inc(v_stored, 16)

            def store_k(L, g):
                if L == DIFF:
                    sp.wait_ge(rope_done, val(g * 2 + 1))
                else:
                    sp.wait_ge(ps_read, val(g * 3 + (N_LAYER * L + 1)))
                sp.dma_start(rows(k_out[L], g), kf[:, 0:T]).then_inc(k_stored, 16)

            def load_vpast(L, g):
                if some(g + G * L):
                    sp.wait_ge(vh_done, val(g + G * L))
                if some(g + G * L):
                    sp.wait_ge(vl_done, val(g + G * L))
                if g.it is None or g.k == 0:
                    src = v_past[L * G + g.c]
                else:
                    src = v_past[bass.ds((g + L * G).v(), 1)].rearrange("a p n -> (a p) n")
                sp.dma_start(vr[:, 5:7, :], src.rearrange("p (b n) -> p b n", b=2)).then_inc(vpast_loaded, 16)

            def load_kpast(L, g):
                if some(g + G * L):
                    sp.wait_ge(kh_done, val(g + G * L))
                if some(g + G * L):
                    sp.wait_ge(kl_done, val(g + G * L))
                sp.dma_start(kf[:, TQ:TK], rows(k_past, g + L * G)).then_inc(kpast_loaded, 16)

            def group(L, g, first=False, second=False):
                u = g * 3 + U_LAYER * L
                start = first and L == DIFF
                if not start:
                    load_unit(u)
                if not first:
                    if not second:
                        store_v(L, g - 2)
                    load_vpast(L, g - 1)
                if second and L == FOX:
                    sp.wait_ge(f_step, 5)
                    sp.dma_start(lf_out, lf[0:2 * G, 0:T]).then_inc(lf_stored, 16)
                if not start:
                    load_unit(u + 1)
                if not first:
                    store_k(L, g - 1)
                elif L == FOX:
                    sp.wait_ge(w_used, val(U_LAYER))
                    sp.dma_start(f_raw[:], w_forget.rearrange("p (k n) -> p k n", n=P)).then_inc(f_loaded, 16)
                    sp.dma_start(upper[:], cst[:, 2 * P + 2 * G:]).then_inc(upper_loaded, 16)
                    sp.dma_start(lft[:, 5:7, :], f_past.rearrange("p (b n) -> p b n", b=2)).then_inc(fpast_loaded, 16)
                load_kpast(L, g)
                load_unit(u + 2)

            load_unit(Num(0))
            sp.dma_start(smalls[:], small).then_inc(small_loaded, 16)
            for k in range(KT):
                sp.dma_start(xT[:, k, :], x_in[P * k:P * (k + 1), :]).then_inc(x_loaded[k], 16)
                if k == 4:
                    load_unit(Num(1))
            sp.dma_start(cstf[:], cst[:, 0:2 * P + 2 * G]).then_inc(cst_loaded, 16)
            sp.dma_start(csth[:], cst16).then_inc(cst_loaded, 16)
            sp.dma_start(cosr[:], rope_tab[:, 0:T]).then_inc(rope_loaded, 16)
            sp.dma_start(sinr[:], rope_tab[:, T:2 * T]).then_inc(rope_loaded, 16)
            for L in (DIFF, FOX):
                group(L, Num(0), first=True)
                group(L, Num(1), second=True)
                with sp.Fori(0, 3) as it:
                    for par in range(2):
                        group(L, Num(2 + par, 2, it))
                for n in range(KT):
                    load_unit(Num(U_LAYER * L + U_WO + n))
                    if n == 0:
                        store_v(L, Num(6))
                        load_vpast(L, Num(7))
                    if n == 1:
                        store_k(L, Num(7))
                    if n == 2:
                        store_v(L, Num(7))
                with sp.Fori(0, FT) as it:
                    for s in range(2):
                        load_unit(Num(U_LAYER * L + U_IN + s, 2, it))
                with sp.Fori(0, KT // 2) as it:
                    for s in range(6):
                        load_unit(Num(U_LAYER * L + U_OUT + s, 6, it), OUT_PARTS[s % 3])
            for k in range(KT):
                sp.wait_ge(y_done, val(k + 1))
                sp.dma_start(y_out[P * k:P * (k + 1), :], yt[:, k, :]).then_inc(y_stored, 16)
            sp.wait_ge(y_stored, 16 * KT)
            sp.wait_ge(k_stored, 16 * 2 * G)
            sp.wait_ge(v_stored, 16 * 2 * G)
            sp.wait_ge(lf_stored, 16)

        @block.tensor
        def _(pe):
            def slice_(u, n, k, rhs_hi, rhs_lo, kt, start, stop):
                slot, out = u.c % 2, proj(n.c % 2)
                for w, rhs in ((w_hi[slot], rhs_hi), (w_hi[slot], rhs_lo), (w_lo[slot], rhs_hi)):
                    for half in range(2):
                        mm = nc.tensor.matmul(out[:, half, :], w[:, k, :], rhs[:, kt, half * HALF:(half + 1) * HALF],
                                              start=start and w is w_hi[slot] and rhs is rhs_hi,
                                              stop=stop and w is w_lo[slot])
                return mm

            def open_unit(u, n=None, tile=True, swapped=None):
                pe.wait_ge(w_hi_done, val(u + 1))
                if u.it is None and u.c == 0:
                    pe.wait_ge(w_lo_first, 1)
                else:
                    pe.wait_ge(w_lo_done, val(u + 1))
                if tile:
                    if some(n - 1):
                        pe.wait_ge(ps_read, val(n - 1))
                    if swapped is not None:
                        pe.wait_ge(ps_swapped, val(swapped))

            def norm_sum(i):
                pe.wait_ge(acc_done, val(KT * (i + 1)))
                for half in range(2):
                    mm = nc.tensor.matmul(sps[:, half, 0:HALF], ones, acc[:, half * HALF:(half + 1) * HALF],
                                          start=True, stop=True)
                mm.then_inc(ss_done, 1)

            def first_unit(u, n, prep, norm):
                open_unit(u, n)
                for k in range(KT):
                    pe.wait_ge(xh_done, val(prep + k + 1))
                    pe.wait_ge(xl_done, val(prep + k + 1))
                    if k == KT // 2 and u.c == 0:
                        pe.wait_ge(w_lo_done, 1)
                    if k == 6 and norm > 0:
                        norm_sum(norm)
                    mm = slice_(u, n, k, xh, xl, k, k == 0, k == KT - 1)
                return mm

            def score(L, a, par, jj):
                i, h = JOBS[L][jj]
                J = (a + G * L) * 10 + jj
                b = slice(64 * h, 64 * h + 64)
                out = sps[:, jj % 2, 0:width(i)]
                q = slice(P * i, P * i + P)
                k = slice(SEQ, TK) if i == 4 else slice(0, width(i))
                if some(J - 1):
                    pe.wait_ge(exp_done, val(J - 1))
                if jj == 0:
                    for s in (qh_done, ql_done, kh_done, kl_done):
                        pe.wait_ge(s, val(a + (G * L + 1)))
                nc.tensor.matmul(out, qh[par][b, q], kh[par][b, k], start=True, stop=False)
                nc.tensor.matmul(out, qh[par][b, q], kl[par][b, k], start=False, stop=False)
                nc.tensor.matmul(out, ql[par][b, q], kh[par][b, k], start=False, stop=False)
                if L == FOX:
                    pe.wait_ge(aug_l_done, val(a * 2 + (h + 1)))
                    nc.tensor.matmul(out, aug_l[h][:, q], aug_r[:, k], start=False, stop=False)
                d = 0 if i == 4 else i
                nc.tensor.matmul(sps[:, jj % 2, P * d:P * d + P], ident16, mask[L], start=False, stop=True
                                 ).then_inc(s_done, 1)

            def transpose_p(L, a, par, tt):
                jj = 2 * tt if L == DIFF else tt
                i, h = JOBS[L][jj]
                tau = t_index(L, a, tt)
                slot = (10 * par + jj) % 4
                pe.wait_ge(p_ready, val(tau + 1))
                if some(tau):
                    pe.wait_ge(pt_lo, val(tau))
                for b in range(width(i) // P):
                    mm = nc.tensor.transpose(tps[:, b, :], pr[:, slot, P * b:P * b + P], ident)
                mm.then_inc(t_done, 1)

            def transpose_v(L, a):
                pe.wait_ge(ps_read, val(a * 3 + (N_LAYER * L + 3)))
                if some(t_index(L, a, 0)):
                    pe.wait_ge(pt_lo, val(t_index(L, a, 0)))
                if some(v_index(L, a, 0)):
                    pe.wait_ge(op_hi, val(v_index(L, a, 0)))
                if L == FOX:
                    if some(a * 2):
                        pe.wait_ge(op_lo, val(a * 2))
                for b in range(4):
                    nc.tensor.transpose(tps[:, b, :], vf[:, P * b:P * b + P], ident)
                nc.tensor.transpose(ops[:, 0:P], vf[:, SEQ:TQ], ident).then_inc(vt_done, 1)

            def pv_sample(L, a, h):
                tt = 0 if L == DIFF else 5 * h
                pe.wait_ge(pt_lo, val(t_index(L, a, tt) + 1))
                pe.wait_ge(vh_done, val(a + (G * L + 1)))
                pe.wait_ge(vl_done, val(a + (G * L + 1)))
                if some(v_index(L, a, h)):
                    pe.wait_ge(op_hi, val(v_index(L, a, h)))
                if L == FOX:
                    if some(a * 2 + h):
                        pe.wait_ge(op_lo, val(a * 2 + h))
                elif later(a):
                    pe.wait_ge(oln_done, val(a))
                wide, narrow = (vh, 2 * NEW), (vl, NEW)
                for b, blk, terms in ((0, 4, (wide, narrow)), (1, 5, (wide, narrow)), (2, 6, (narrow, wide))):
                    for v, n in terms:
                        mm = nc.tensor.matmul(ops[:, 0:n], v[:, blk, :], pts[:, b, 0:n],
                                              start=b == 0 and v is vh, stop=b == 2 and v is vh)
                mm.then_inc(pvs_done, 1)

            def pv_prompt(L, a, h):
                tt = 4 if L == DIFF else 5 * h + 4
                pe.wait_ge(pt_lo, val(t_index(L, a, tt) + 1))
                pe.wait_ge(os_taken, val(v_index(L, a, h) + 1))
                for j in range(4):
                    for v, p in ((vh, pth), (vh, ptl), (vl, pth)):
                        mm = nc.tensor.matmul(ops[:, P * j:SEQ], v[:, j, :], p[:, j, P * j:SEQ],
                                              start=j == 0 and v is vh and p is pth, stop=j == 3 and v is vl)
                mm.then_inc(pvp_done, 1)

            def head_norm_sum(a):
                pe.wait_ge(osq_done, val(a + 1))
                nc.tensor.matmul(ops[:], ones, osq[:, 0:SEQ], start=True, stop=True)
                nc.tensor.matmul(tps[:, 0, 0:NEW], ones, osq[:, SEQ:T], start=True, stop=True).then_inc(oss_done, 1)

            def attention(L, a, par, slot, first=False):
                if slot == 0 and not first:
                    pv_prompt(L, a - 1, L)
                if slot == VT_AT:
                    transpose_v(L, a)
                if slot == SS_AT and L == DIFF and not first:
                    pe.wait_ge(vr_done, val((a + 1) * 2))
                    head_norm_sum(a - 1)
                for jj in range(10):
                    if S_AT[L][jj] == slot:
                        score(L, a, par, jj)
                for tt in range(len(T_AT[L])):
                    if T_AT[L][tt] == slot:
                        if tt == 0:
                            pe.wait_ge(vr_done, val((a + (G * L + 1)) * 2))
                            if L == DIFF and not first:
                                pe.wait_ge(oln_done, val(a))
                        transpose_p(L, a, par, tt)
                for h in range(len(PVS_AT[L])):
                    if PVS_AT[L][h] == slot:
                        pv_sample(L, a, h)
                    if PVP_AT[L][h] == slot:
                        pv_prompt(L, a, h)

            def group(L, g, par, first=False):
                u, n = g * 3 + U_LAYER * L, g * 3 + N_LAYER * L
                lag = 1 if first else 0
                for slot in range(SLOTS):
                    if slot >= lag:
                        attention(L, g - 1, 1 - par, slot - lag, first)
                    part, k = slot // KT, slot % KT
                    if k == 0:
                        swapped = None
                        if L == DIFF:
                            swapped = (g * 2, g * 2, g * 2 + 1)[part]
                        open_unit(u + part, n + part, swapped=swapped)
                    mm = slice_(u + part, n + part, k, xh, xl, k, k == 0, k == KT - 1)
                    if k == KT - 1:
                        mm.then_inc(w_used, 1)
                for slot in range(SLOTS - lag, SLOTS):
                    attention(L, g - 1, 1 - par, slot, first)

            def first_group(L):
                u, n = Num(U_LAYER * L), Num(N_LAYER * L)
                first_unit(u, n, prep_count(L, 0, 0), 2 * L).then_inc(w_used, 1)
                if L == FOX:
                    pe.wait_ge(f_hi_done, 1)
                    pe.wait_ge(f_lo_done, 1)
                    pe.wait_ge(r_ready, 3)
                    for k in range(KT):
                        for w, rhs in ((f_hi, xh), (f_hi, xl), (f_lo, xh)):
                            for half in range(2):
                                mm = nc.tensor.matmul(sps[:, half, 0:HALF], w[:, k, :],
                                                      rhs[:, k, half * HALF:(half + 1) * HALF],
                                                      start=k == 0 and w is f_hi and rhs is xh,
                                                      stop=k == KT - 1 and w is f_lo)
                    mm.then_inc(f_proj, 1)
                for part in (1, 2):
                    if part == 2 and L == FOX:
                        forget_cumsum()
                    open_unit(u + part, n + part, swapped=1 if L == DIFF and part == 2 else None)
                    for k in range(KT):
                        if L == DIFF and part == 1 and k == NORM0_AT:
                            pe.wait_ge(cst_loaded, 32)
                            norm_sum(0)
                        mm = slice_(u + part, n + part, k, xh, xl, k, k == 0, k == KT - 1)
                    mm.then_inc(w_used, 1)

            def forget_cumsum():
                pe.wait_ge(f_step, 5)
                for b in range(4):
                    nc.tensor.transpose(tps[:, b, :], lf[:, P * b:P * b + P], ident)
                nc.tensor.transpose(ops[:, 0:P], lf[:, SEQ:TQ], ident).then_inc(f_tr, 1)
                pe.wait_ge(f_lt, 2)
                pe.wait_ge(fpast_loaded, 16)
                pe.wait_ge(upper_loaded, 16)
                for b in range(4):
                    nc.tensor.matmul(sps[:, 0, P * b:SEQ], lft[:, b, :], upper[:, 0:SEQ - P * b],
                                     start=b == 0, stop=b == 3)
                for b, blk in enumerate((5, 6, 4)):
                    mm = nc.tensor.matmul(sps[:, 1, P * b:3 * P], lft[:, blk, :], upper[:, 0:3 * P - P * b],
                                          start=b == 0, stop=b == 2)
                mm.then_inc(f_cum, 1)

            def last_attention(L, par):
                a = Num(7)
                u, n = U_LAYER * L + U_WO, N_LAYER * L + N_WO

                def wo(q):
                    j, tile, k = WO_STEPS[q]
                    if q % KT == 0:
                        open_unit(Num(u + q // KT), tile=False)
                    if q == WO_OPEN[j]:
                        pe.wait_ge(ps_read, n + j - 1)
                        if L == DIFF and j < 2:
                            pe.wait_ge(ps_swapped, 2 * G)
                    if j == 0 or k == KT - 1:
                        if L == DIFF:
                            pe.wait_ge(oh_done, k + 1)
                            pe.wait_ge(ol_done, k + 1)
                        else:
                            pe.wait_ge(op_lo, 2 * k + 2)
                    mm = slice_(Num(u + q // KT), Num(n + j), q % KT, oh, ol, k, q == WO_OPEN[j], q == WO_END[j])
                    if q % KT == KT - 1:
                        mm.then_inc(w_used, 1)
                    elif q == WO_END[j]:
                        mm.then_inc(wo_done, 1)

                for slot in range(SLOTS):
                    attention(L, a, par, slot)
                    wo(slot)
                for q in range(SLOTS, len(WO_STEPS)):
                    if q == SLOTS + LAST_PV:
                        pv_prompt(L, a, L)
                    if L == DIFF and q == SLOTS + 7:
                        head_norm_sum(a)
                    wo(q)

            for L in (DIFF, FOX):
                first_group(L)
                group(L, Num(1), 1, first=True)
                with pe.Fori(0, 3) as it:
                    for par in range(2):
                        group(L, Num(2 + par, 2, it), par)
                last_attention(L, 1)
                u, n = Num(U_LAYER * L + U_IN), Num(N_LAYER * L + N_IN)
                first_unit(u, n, prep_count(L, 1, 0), 2 * L + 1).then_inc(w_used, 1)
                open_unit(u + 1, n + 1)
                for k in range(KT):
                    mm = slice_(u + 1, n + 1, k, xh, xl, k, k == 0, k == KT - 1)
                mm.then_inc(w_used, 1)
                with pe.Fori(0, FT - 1) as it:
                    for s in range(2):
                        ui, ni = Num(u.c + 2 + s, 2, it), Num(n.c + 2 + s, 2, it)
                        open_unit(ui, ni)
                        for k in range(KT):
                            mm = slice_(ui, ni, k, xh, xl, k, k == 0, k == KT - 1)
                        mm.then_inc(w_used, 1)

                def out_tile(u, n, first):
                    for part, kts in enumerate(OUT_PARTS):
                        open_unit(u + part, n, tile=part == 0)
                        for k in range(kts):
                            kt = KT * part + k
                            if first:
                                pe.wait_ge(hl_done, val(FT * L + kt + 1))
                            mm = slice_(u + part, n, k, hh, hl, kt, kt == 0, kt == FT - 1)
                        mm.then_inc(w_used, 1)

                u, n = Num(U_LAYER * L + U_OUT), Num(N_LAYER * L + N_OUT)
                out_tile(u, n, True)
                out_tile(u + 3, n + 1, False)
                with pe.Fori(0, 3) as it:
                    for s in range(2):
                        out_tile(Num(u.c + 6 + 3 * s, 6, it), Num(n.c + 2 + s, 2, it), False)
            norm_sum(4)

        def unit_done(L, n):
            return n + U_LAYER * L + 1

        @block.scalar
        def _(act):
            def apart():
                act.wait_ge(small_loaded, 16)

            def split(u, kts=KT):
                slot = u.c % 2
                act.wait_ge(w_loaded[slot], val((u.half() + 1) * 16))
                if some(u - 1):
                    act.wait_ge(w_used, val(u - 1))
                nc.scalar.activation(w_hi[slot][:, 0:kts, :], w_raw[slot][:, 0:kts, :], ACT.Copy
                                     ).then_inc(w_hi_done, 1)

            def lead(u, kts=KT):
                split(u + 1, kts)

            def column(tile, n):
                if n.it is None or n.k == 0:
                    return tile[:, n.c:n.c + 1]
                return tile[:, bass.ds(n.v(), 1)]

            def prep(i, n):
                if n.it is not None:
                    act.wait_ge(acc_done, val(n + KT * i))
                    apart()
                if i < 4:
                    nc.scalar.activation(at(xh, n), at(xT, n), ACT.Copy, scale=column(norm_w[i], n)
                                         ).then_inc(xh_done, 1)
                if n.it is None:
                    act.wait_ge(acc_done, val(n + KT * i))
                nc.scalar.activation(sqt[:], at(xT, n), ACT.Square).then_inc(sq_done, 1)

            def scale_of_norm(i):
                act.wait_ge(ss_done, val(i + 1))
                nc.scalar.activation(halves(rs[:]), sps[:, :, 0:HALF], ACT.Ln, bias=eps[:, 0:1], scale=1.0 / D
                                     ).then_inc(ln_done, 1)
                act.wait_ge(ln_done, val(i + 1))
                nc.scalar.activation(rs[:], rs[:], ACT.Exp, scale=-0.5).then_inc(r_ready, 1)

            def swap(g, n, which, quadrants):
                act.wait_ge(ps_read, val(n + 1))
                if some(g * 2 + which):
                    act.wait_ge(rope_done, val(g * 2 + which))
                src = proj(n.c % 2)
                for q in quadrants:
                    o = q ^ 1
                    mv = nc.scalar.activation(halves(qsw[32 * q:32 * q + 32, :]), src[32 * o:32 * o + 32], ACT.Copy)
                if 3 in quadrants:
                    mv.then_inc(ps_swapped, 1)

            def k_hi(L, g, par):
                act.wait_ge(kpast_loaded, val((g + (G * L + 1)) * 16))
                act.wait_ge(pads_zero, val(6 * (L + 1)))
                if some((g + (G * L - 1)) * 10):
                    act.wait_ge(s_done, val((g + (G * L - 1)) * 10))
                if L == DIFF:
                    act.wait_ge(rope_done, val(g * 2 + 1))
                else:
                    act.wait_ge(ps_read, val(g * 3 + (N_LAYER * L + 1)))
                nc.scalar.activation(kh[par][:], kf[:], ACT.Copy).then_inc(kh_done, 1)

            def q_hi(L, g, par):
                if L == DIFF:
                    act.wait_ge(rope_done, val(g * 2 + 2))
                else:
                    act.wait_ge(ps_read, val(g * 3 + (N_LAYER * L + 2)))
                if some((g + (G * L - 1)) * 10):
                    act.wait_ge(s_done, val((g + (G * L - 1)) * 10))
                nc.scalar.activation(qh[par][:, 0:T], qf[:], ACT.Copy, scale=QK_SCALE).then_inc(qh_done, 1)

            def take_v(L, a):
                gi = a + G * L
                act.wait_ge(vt_done, val(gi + 1))
                if some(gi):
                    act.wait_ge(vl_done, val(gi))
                if some(gi):
                    act.wait_ge(vh_done, val(gi))
                nc.scalar.activation(vr[:, 0:4, :], tps[:], ACT.Copy).then_inc(vr_done, 1)
                nc.scalar.activation(vr[:, 4, :], ops[:, 0:P], ACT.Copy).then_inc(vr_done, 1)
                act.wait_ge(vr_done, val((gi + 1) * 2))
                act.wait_ge(vpast_loaded, val((gi + 1) * 16))
                if some(v_index(L, a, 0)):
                    act.wait_ge(pvp_done, val(v_index(L, a, 0)))
                nc.scalar.activation(vh[:], vr[:], ACT.Copy).then_inc(vh_done, 1)

            def exps(L, a, par, jj):
                i, h = JOBS[L][jj]
                J = (a + G * L) * 10 + jj
                slot = (10 * par + jj) % 4
                act.wait_ge(max_done, val(J + 1))
                if L == DIFF:
                    if some(a * 5 + ((jj - 4) // 2 + 1)):
                        act.wait_ge(t_done, val(a * 5 + ((jj - 4) // 2 + 1)))
                elif later(a) or jj >= 4:
                    act.wait_ge(t_done, val(a * 10 + (5 * G + jj - 3)))
                nc.scalar.activation(pr[:, slot, 0:width(i)], sps[:, jj % 2, 0:width(i)], ACT.Exp,
                                     bias=nmax[:, slot:slot + 1], accum_out=den[:, slot:slot + 1]
                                     ).then_inc(exp_done, 1)

            def take_p(L, a, tt):
                i, h = JOBS[L][2 * tt if L == DIFF else tt]
                tau = t_index(L, a, tt)
                act.wait_ge(t_done, val(tau + 1))
                if i == 4:
                    if some(v_index(L, a, h if L == FOX else 0)):
                        act.wait_ge(pvs_done, val(v_index(L, a, h if L == FOX else 0)))
                    dst, src = pts[:, :, 0:NEW], tps[:, 0:3, 0:NEW]
                else:
                    if some(v_index(L, a, h if L == FOX else 0)):
                        act.wait_ge(pvp_done, val(v_index(L, a, h if L == FOX else 0)))
                    dst, src = pth[:, 0:i + 1, P * i:P * i + P], tps[:, 0:i + 1, :]
                nc.scalar.activation(dst, src, ACT.Copy).then_inc(pt_hi, 1)

            def take_o_sample(L, a, h):
                act.wait_ge(pvs_done, val(v_index(L, a, h) + 1))
                if some(v_index(L, a, h)):
                    act.wait_ge(os_summed, val(v_index(L, a, h)))
                nc.scalar.activation(os2[:], ops[:, 0:2 * NEW], ACT.Copy).then_inc(os_taken, 1)

            def o_hi_sample(a, h):
                r = slice(64 * h, 64 * h + 64)
                act.wait_ge(os_summed, val(v_index(FOX, a, h) + 1))
                act.wait_ge(lf_stored, 16)
                nc.scalar.activation(at_cols(oh, a, r, slice(SEQ, T)), osum[r, :], ACT.Copy).then_inc(os_hi, 1)

            def take_o(L, a, h):
                act.wait_ge(pvp_done, val(v_index(L, a, h) + 1))
                if L == DIFF:
                    nc.scalar.activation(og[:, 0:SEQ], ops[:], ACT.Copy).then_inc(op_hi, 1)
                else:
                    r = slice(64 * h, 64 * h + 64)
                    act.wait_ge(lf_stored, 16)
                    nc.scalar.activation(at_cols(oh, a, r, slice(0, SEQ)), ops[r, :], ACT.Copy).then_inc(op_hi, 1)

            def head_scale(a):
                act.wait_ge(oss_done, val(a + 1))
                act.wait_ge(on_done, val(a + 1))
                nc.scalar.activation(ors[:, 0:SEQ], ops[:], ACT.Ln, bias=eps[:, 1:2], scale=1.0 / P)
                nc.scalar.activation(ors[:, SEQ:T], tps[:, 0, 0:NEW], ACT.Ln, bias=eps[:, 1:2], scale=1.0 / P
                                     ).then_inc(oln_done, 1)
                act.wait_ge(oln_done, val(a + 1))
                nc.scalar.activation(ors[:], ors[:], ACT.Exp, scale=-0.5).then_inc(ors_done, 1)

            def o_hi(a):
                act.wait_ge(on_done, val(a + 2))
                apart()
                nc.scalar.activation(at(oh, a), og[:], ACT.Copy).then_inc(oh_done, 1)

            def attention(L, a, par, slot, first=False):
                if slot == 0 and not first:
                    take_o(L, a - 1, L)
                if slot == VT_AT + 1:
                    take_v(L, a)
                if L == DIFF and not first:
                    if slot == SS_AT:
                        head_scale(a - 1)
                    if slot == SS_AT + 3:
                        o_hi(a - 1)
                for jj in range(10):
                    if S_AT[L][jj] == slot:
                        exps(L, a, par, jj)
                for tt in range(len(T_AT[L])):
                    if T_AT[L][tt] == slot:
                        take_p(L, a, tt)
                for h in range(len(PVS_AT[L])):
                    if PVS_AT[L][h] == slot:
                        take_o_sample(L, a, h)
                    if PVP_AT[L][h] == slot:
                        take_o(L, a, h)
                    if L == FOX and PVS_AT[L][h] + 1 == slot:
                        o_hi_sample(a, h)

            def group(L, g, par, first=False, alone=False):
                u, n = g * 3 + U_LAYER * L, g * 3 + N_LAYER * L
                for slot in range(SLOTS):
                    if not alone:
                        attention(L, g - 1, 1 - par, slot, first)
                    if alone and L == FOX and slot == 0:
                        act.wait_ge(f_loaded, 16)
                        nc.scalar.activation(f_hi[:], f_raw[:], ACT.Copy).then_inc(f_hi_done, 1)
                        scale_of_norm(2)
                    if alone and L == DIFF and slot == 0:
                        scale_of_norm(0)
                    if alone and L == FOX and slot == 13:
                        forget()
                    if slot == 8:
                        lead(u + 1)
                    if slot == SWAP_AT[0] and L == DIFF:
                        swap(g, n, 0, range(4))
                    if slot == K_HI_AT[L]:
                        k_hi(L, g, par)
                    if slot == SWAP_AT[1] and L == DIFF:
                        swap(g, n + 1, 1, (0, 1))
                    if slot == SWAP_AT[1] + 1 and L == DIFF:
                        swap(g, n + 1, 1, (2, 3))
                    if slot == LEAD_AT[L]:
                        lead(u + 2)
                    if slot == Q_AT[L]:
                        q_hi(L, g, par)
                lead(u + 3)

            def forget():
                act.wait_ge(f_step, 4)
                nc.scalar.activation(fe[:], fe[:], ACT.Exp, scale=-1.0).then_inc(f_exp, 1)
                act.wait_ge(f_exp, 1)
                nc.scalar.activation(fe[:], fe[:], ACT.Ln, bias=ones[:, 0:1]).then_inc(f_ln, 1)
                act.wait_ge(f_tr, 1)
                nc.scalar.activation(lft[:, 0:4, :], tps[:], ACT.Copy).then_inc(f_lt, 1)
                nc.scalar.activation(lft[:, 4, :], ops[:, 0:P], ACT.Copy).then_inc(f_lt, 1)
                act.wait_ge(f_step, 8)
                nc.scalar.activation(cumh[:], cum[:], ACT.Copy).then_inc(cum_hi, 1)

            act.preload_act_table_set("natural_log_exp_and_others")
            split(Num(0))
            act.wait_ge(eps_set, 2)
            act.wait_ge(small_loaded, 16)
            for k in range(KT):
                act.wait_ge(x_loaded[k], 16)
                nc.scalar.activation(xh[:, k, :], xT[:, k, :], ACT.Copy, scale=norm_w[0][:, k:k + 1]
                                     ).then_inc(xh_done, 1)
                if k % 2 or k == 6:
                    nc.scalar.activation(sq_all[:, k, :], xT[:, k, :], ACT.Square).then_inc(sq_act, 1)
                if k == 6:
                    lead(Num(0))
            act.wait_ge(lam_step, 2)
            nc.scalar.activation(nlam[:, 2:4], nlam[:, 0:2], ACT.Exp).then_inc(lam_exp, 1)
            for L in (DIFF, FOX):
                group(L, Num(0), 0, alone=True)
                group(L, Num(1), 1, first=True)
                with act.Fori(0, 3) as it:
                    for par in range(2):
                        group(L, Num(2 + par, 2, it), par)
                u = Num(U_LAYER * L + U_WO)
                for slot in range(SLOTS):
                    attention(L, Num(7), 1, slot)
                    if slot in (KT + 2, 2 * KT + 2):
                        lead(u + slot // KT)
                lead(u + 3)
                take_o(L, Num(7), L)
                if L == DIFF:
                    head_scale(Num(7))
                lead(u + 4)
                if L == DIFF:
                    o_hi(Num(7))
                lead(u + 5)
                for k in range(KT):
                    act.wait_ge(ps_read, N_LAYER * L + N_WO + 4 + k + 1)
                    prep(2 * L + 1, Num(k))
                    if k == 0:
                        lead(u + 6)
                    if k == 4:
                        lead(u + 7)
                lead(u + 8)
                scale_of_norm(2 * L + 1)

                def gate_up(jt):
                    j = jt + FT * L
                    u, n = jt * 2 + (U_LAYER * L + U_IN), jt * 2 + (N_LAYER * L + N_IN)
                    lead(u + 1)
                    act.wait_ge(ps_read, val(n + 1))
                    if some(j):
                        act.wait_ge(hf_done, val(j))
                    nc.scalar.activation(sg[:], gf[:], ACT.Silu).then_inc(sg_done, 1)
                    lead(u + 2)
                    act.wait_ge(hf_done, val(j + 1))
                    apart()
                    nc.scalar.activation(at(hh, jt), hf[:], ACT.Copy).then_inc(hh_done, 1)

                gate_up(Num(0))
                with act.Fori(0, FT - 1) as it:
                    gate_up(Num(1, 1, it))
                act.preload_act_table_set("natural_log_exp_and_others")

                def out_tile(n, u, last):
                    lead(u + 1, OUT_PARTS[2])
                    if not last:
                        lead(u + 2)
                        lead(u + 3)
                    act.wait_ge(ps_read, val(n + (N_LAYER * L + N_OUT + 1)))
                    prep(2 * L + 2, n)

                u = U_LAYER * L + U_OUT
                with act.Fori(0, KT // 2 - 1) as it:
                    for s in range(2):
                        out_tile(Num(s, 2, it), Num(u + 3 * s, 6, it), False)
                for n in range(KT - 2, KT):
                    out_tile(Num(n), Num(u + 3 * n), L == FOX and n == KT - 1)
            scale_of_norm(4)

        @block.gpsimd
        def _(pool):
            def lead(u, kts=KT):
                u = u + 1
                slot = u.c % 2
                pool.wait_ge(w_hi_done, val(u + 1))
                if some(u - 1):
                    pool.wait_ge(w_used, val(u - 1))
                nc.gpsimd.tensor_tensor(w_lo[slot][:, 0:kts, :], w_raw[slot][:, 0:kts, :],
                                        w_hi[slot][:, 0:kts, :].bitcast(F32), ALU.subtract).then_inc(w_lo_done, 1)

            def times_sin(g, which):
                pool.wait_ge(ps_swapped, val(g * 2 + (which + 1)))
                nc.gpsimd.tensor_tensor(qsw[:], qsw[:], sinr[:], ALU.mult).then_inc(part_done, 1)

            def v_lo(L, a):
                pool.wait_ge(vh_done, val(a + (G * L + 1)))
                nc.gpsimd.tensor_tensor(vl[:], vr[:], vh[:].bitcast(F32), ALU.subtract).then_inc(vl_done, 1)

            def o_square(a):
                pool.wait_ge(op_hi, val(a + 1))
                pool.wait_ge(os_summed, val(a + 1))
                nc.gpsimd.tensor_tensor(osq[:], og[:], og[:], ALU.mult).then_inc(osq_done, 1)

            def group(L, g, alone=False, first=False):
                u = g * 3 + U_LAYER * L
                if L == DIFF and not alone and not first:
                    o_square(g - 2)
                if alone and L == FOX:
                    pool.wait_ge(f_hi_done, 1)
                    nc.gpsimd.tensor_tensor(f_lo[:], f_raw[:], f_hi[:].bitcast(F32), ALU.subtract
                                            ).then_inc(f_lo_done, 1)
                if not alone:
                    v_lo(L, g - 1)
                lead(u + 1)
                if L == DIFF:
                    if alone:
                        pool.wait_ge(rope_scaled, 2)
                    times_sin(g, 0)
                    times_sin(g, 1)
                lead(u + 2)
                lead(u + 3)

            pool.wait_ge(w_hi_done, 1)
            nc.gpsimd.tensor_tensor(w_lo[0][:, KT // 2:KT, :], w_raw[0][:, KT // 2:KT, :],
                                    w_hi[0][:, KT // 2:KT, :].bitcast(F32), ALU.subtract).then_inc(w_lo_done, 1)
            for k in (0, 2, 4):
                pool.wait_ge(x_loaded[k], 16)
                nc.gpsimd.tensor_tensor(sq_all[:, k, :], xT[:, k, :], xT[:, k, :], ALU.mult).then_inc(sq_pool, 1)
            lead(Num(0))
            for L in (DIFF, FOX):
                group(L, Num(0), alone=True)
                group(L, Num(1), first=True)
                with pool.Fori(0, 3) as it:
                    for par in range(2):
                        group(L, Num(2 + par, 2, it))
                if L == DIFF:
                    o_square(Num(6))
                v_lo(L, Num(7))
                for n in range(1, KT + 1):
                    if L == DIFF and n == 4:
                        o_square(Num(7))
                    lead(Num(U_LAYER * L + U_WO + n))

                def gate_up(jt):
                    j = jt + FT * L
                    u, n = jt * 2 + (U_LAYER * L + U_IN), jt * 2 + (N_LAYER * L + N_IN)
                    lead(u + 1)
                    lead(u + 2)
                    pool.wait_ge(sg_done, val(j + 1))
                    pool.wait_ge(ps_read, val(n + 2))
                    if some(j):
                        pool.wait_ge(hl_done, val(j))
                    nc.gpsimd.tensor_tensor(hf[:], sg[:], uf[:], ALU.mult).then_inc(hf_done, 1)

                gate_up(Num(0))
                with pool.Fori(0, FT - 1) as it:
                    gate_up(Num(1, 1, it))
                u = U_LAYER * L + U_OUT
                with pool.Fori(0, KT // 2 - 1) as it:
                    for s in range(2):
                        ut = Num(u + 3 * s, 6, it)
                        lead(ut + 1, OUT_PARTS[2])
                        lead(ut + 2)
                        lead(ut + 3)
                for n in range(KT - 2, KT):
                    lead(Num(u + 3 * n + 1), OUT_PARTS[2])
                    if L == DIFF or n < KT - 1:
                        lead(Num(u + 3 * n + 2))
                        lead(Num(u + 3 * n + 3))

        @block.vector
        def _(dve):
            tt = nc.vector.tensor_tensor
            stt = nc.vector.scalar_tensor_tensor

            def column(tile, n):
                if n.it is None or n.k == 0:
                    return tile[:, n.c:n.c + 1]
                return tile[:, bass.ds(n.v(), 1)]

            def prep(i, n):
                if i < 4:
                    dve.wait_ge(xh_done, val(n + (KT * i + 1)))
                    stt(at(xl, n), at(xT, n), column(norm_w[i], n), at(xh, n).bitcast(F32), ALU.mult, ALU.subtract
                        ).then_inc(xl_done, 1)
                dve.wait_ge(sq_done, val(n + (KT * (i - 1) + 1)))
                if some(n + KT * i):
                    dve.wait_ge(acc_done, val(n + KT * i))
                tt(acc[:], acc[:], sqt[:], ALU.add).then_inc(acc_done, 1)

            def clear_acc(i):
                dve.wait_ge(ss_done, i)
                nc.vector.memset(acc[:], 0.0).then_inc(acc_zero, 1)
                dve.wait_ge(acc_zero, i)

            def residual(n, k):
                tt(halves(at(xT, k)), proj(n.c % 2), halves(at(xT, k)), ALU.add).then_inc(ps_read, 1)
                dve.wait_ge(ps_read, val(n + 1))

            def take(dst, units, n, scale):
                dve.wait_ge(w_used, val(units))
                tt(halves(dst), proj(n.c % 2), halves(scale), ALU.mult).then_inc(ps_read, 1)

            def take_k(L, g):
                gi = g + G * L
                if some(gi * 16):
                    dve.wait_ge(k_stored, val(gi * 16))
                if some(gi):
                    dve.wait_ge(kh_done, val(gi))
                take(kf[:, 0:T], g * 3 + (U_LAYER * L + 1), g * 3 + N_LAYER * L, (cosr if L == DIFF else rs)[:])

            def take_q(L, g):
                if some(g + G * L):
                    dve.wait_ge(qh_done, val(g + G * L))
                take(qf[:], g * 3 + (U_LAYER * L + 2), g * 3 + (N_LAYER * L + 1), (cosr if L == DIFF else rs)[:])

            def take_v(L, g):
                gi = g + G * L
                if some(gi):
                    dve.wait_ge(vt_done, val(gi))
                if some(gi * 16):
                    dve.wait_ge(v_stored, val(gi * 16))
                take(vf[:, 0:T], g * 3 + (U_LAYER * L + 3), g * 3 + (N_LAYER * L + 2), rs[:])

            def rotate(g, which):
                x = (kf, qf)[which]
                dve.wait_ge(part_done, val(g * 2 + (which + 1)))
                dve.wait_ge(ps_read, val(g * 3 + (which + 1)))
                tt(x[:, 0:T], x[:, 0:T], qsw[:], ALU.add).then_inc(rope_done, 1)

            def k_lo(L, g, par):
                dve.wait_ge(kh_done, val(g + (G * L + 1)))
                tt(kl[par][:], kf[:], kh[par][:].bitcast(F32), ALU.subtract).then_inc(kl_done, 1)

            def q_lo(L, g, par):
                dve.wait_ge(qh_done, val(g + (G * L + 1)))
                stt(ql[par][:, 0:T], qf[:], QK_SCALE, qh[par][:, 0:T].bitcast(F32), ALU.mult, ALU.subtract
                    ).then_inc(ql_done, 1)

            def row_max(L, a, par, jj):
                i, h = JOBS[L][jj]
                J = (a + G * L) * 10 + jj
                slot = (10 * par + jj) % 4
                dve.wait_ge(s_done, val(J + 1))
                nc.vector.tensor_reduce(nmax[:, slot:slot + 1], sps[:, jj % 2, 0:width(i)], AX_X, ALU.max,
                                        negate=True).then_inc(max_done, 1)

            def weigh(L, a, par, jj):
                i, h = JOBS[L][jj]
                w = width(i)
                tau = t_index(L, a, jj // 2 if L == DIFF else jj)
                dve.wait_ge(exp_done, val((a + G * L) * 10 + (jj + 1)))
                if L == DIFF:
                    sa = (10 * par + jj - 1) % 4
                    s_b = sa + 1
                    nc.vector.reciprocal(rden[:, sa:sa + 2], den[:, sa:sa + 2]).then_inc(rden_done, 1)
                    dve.wait_ge(rden_done, val(tau + 1))
                    tt(nlr[:, s_b:s_b + 1], rden[:, s_b:s_b + 1], nlam[:, 5:6], ALU.mult).then_inc(nlr_done, 1)
                    nc.vector.tensor_scalar(pr[:, sa, 0:w], pr[:, sa, 0:w], rden[:, sa:sa + 1], None, ALU.mult
                                            ).then_inc(pa_done, 1)
                    dve.wait_ge(nlr_done, val(tau + 1))
                    dve.wait_ge(pa_done, val(tau + 1))
                    stt(pr[:, sa, 0:w], pr[:, s_b, 0:w], nlr[:, s_b:s_b + 1], pr[:, sa, 0:w], ALU.mult, ALU.add
                        ).then_inc(p_ready, 1)
                else:
                    s = (10 * par + jj) % 4
                    nc.vector.reciprocal(rden[:, s:s + 1], den[:, s:s + 1]).then_inc(rden_done, 1)
                    dve.wait_ge(rden_done, val(tau + 1))
                    nc.vector.tensor_scalar(pr[:, s, 0:w], pr[:, s, 0:w], rden[:, s:s + 1], None, ALU.mult
                                            ).then_inc(p_ready, 1)

            def p_lo(L, a, tt_):
                i, h = JOBS[L][2 * tt_ if L == DIFF else tt_]
                dve.wait_ge(pt_hi, val(t_index(L, a, tt_) + 1))
                if i == 4:
                    dst, hi, src = pts[:, :, NEW:2 * NEW], pts[:, :, 0:NEW], tps[:, 0:3, 0:NEW]
                else:
                    cols = slice(P * i, P * i + P)
                    dst, hi, src = ptl[:, 0:i + 1, cols], pth[:, 0:i + 1, cols], tps[:, 0:i + 1, :]
                tt(dst, src, hi.bitcast(F32), ALU.subtract).then_inc(pt_lo, 1)

            def o_sum(L, a, h):
                dve.wait_ge(os_taken, val(v_index(L, a, h) + 1))
                tt(og[:, SEQ:T] if L == DIFF else osum[:], os2[:, 0:NEW], os2[:, NEW:2 * NEW], ALU.add
                   ).then_inc(os_summed, 1)

            def o_lo_sample(a, h):
                r, cols = slice(64 * h, 64 * h + 64), slice(SEQ, T)
                dve.wait_ge(os_hi, val(a * 2 + (h + 1)))
                tt(at_cols(ol, a, r, cols), osum[r, :], at_cols(oh, a, r, cols).bitcast(F32), ALU.subtract)

            def o_lo(a, h):
                r, cols = slice(64 * h, 64 * h + 64), slice(0, SEQ)
                dve.wait_ge(op_hi, val(v_index(FOX, a, h) + 1))
                tt(at_cols(ol, a, r, cols), ops[r, :], at_cols(oh, a, r, cols).bitcast(F32), ALU.subtract
                   ).then_inc(op_lo, 1)

            def norm_o(a):
                dve.wait_ge(ors_done, val(a + 1))
                stt(og[:], og[:], sub_w[:], ors[:], ALU.mult, ALU.mult).then_inc(on_done, 1)

            def split_o(a):
                dve.wait_ge(oh_done, val(a + 1))
                tt(at(ol, a), og[:], at(oh, a).bitcast(F32), ALU.subtract).then_inc(ol_done, 1)

            def aug_left(g):
                for h in range(2):
                    if later(g):
                        dve.wait_ge(s_done, val((g + (G - 1)) * 10 + 5 * (h + 1)))
                    nc.vector.tensor_scalar(aug_l[h][:], aug_m[:], column(head_sel, g * 2 + h), None, ALU.mult
                                            ).then_inc(aug_l_done, 1)

            def attention(L, a, par, slot, first=False):
                if slot == 0 and L == FOX and not first:
                    o_lo(a - 1, 1)
                if L == DIFF and not first:
                    if slot == SS_AT + 2:
                        norm_o(a - 1)
                    if slot == SS_AT + 4:
                        split_o(a - 1)
                for jj in range(10):
                    if S_AT[L][jj] == slot:
                        row_max(L, a, par, jj)
                for jj in range(10):
                    if S_AT[L][jj] + 1 == slot and (L == FOX or jj % 2):
                        weigh(L, a, par, jj)
                for t in range(len(T_AT[L])):
                    if T_AT[L][t] == slot:
                        p_lo(L, a, t)
                for h in range(len(PVS_AT[L])):
                    if PVS_AT[L][h] == slot:
                        o_sum(L, a, h)
                    if L == FOX and PVS_AT[L][h] + 2 == slot:
                        o_lo_sample(a, h)
                    if PVP_AT[L][h] == slot:
                        o_lo(a, h)

            def group(L, g, par, first=False, alone=False):
                for slot in range(SLOTS):
                    if not alone:
                        attention(L, g - 1, 1 - par, slot, first)
                    if slot == 8:
                        take_k(L, g)
                    if slot == 9 and alone and L == FOX:
                        forget_1()
                    if slot == ROTATE_AT[0] and L == DIFF:
                        rotate(g, 0)
                    if slot == K_LO_AT[L]:
                        k_lo(L, g, par)
                    if slot == (2 * KT if alone else TAKE_Q_AT[L]):
                        take_q(L, g)
                    if slot == 17 and alone and L == FOX:
                        forget_2()
                    if slot == ROTATE_AT[1] and L == DIFF:
                        rotate(g, 1)
                    if slot == Q_AT[L]:
                        q_lo(L, g, par)
                        if L == FOX:
                            aug_left(g)
                take_v(L, g)

            def forget_1():
                nc.vector.memset(lf[:, T:TQ], 0.0).then_inc(f_step, 1)
                nc.vector.memset(aug_m[0:64, :], 1.0).then_inc(aug_ones, 1)
                nc.vector.memset(aug_r[64:128, :].bitcast(F32), 1.0).then_inc(aug_ones, 1)
                dve.wait_ge(f_proj, 1)
                tt(halves(fz[:]), sps[:, :, 0:HALF], halves(rs[:]), ALU.mult).then_inc(f_step, 1)
                dve.wait_ge(f_step, 2)
                nc.vector.tensor_scalar(fz[:], fz[:], b_f, None, ALU.add).then_inc(f_step, 1)
                dve.wait_ge(f_step, 3)
                stt(fe[:], fz[:], -1.0, fz[:], ALU.mult, ALU.max).then_inc(f_step, 1)
                dve.wait_ge(f_ln, 1)
                stt(lf[:, 0:T], fz[:], 0.0, fe[:], ALU.min, ALU.subtract).then_inc(f_step, 1)

            def forget_2():
                dve.wait_ge(f_cum, 1)
                nc.vector.tensor_copy(cum[:, 0:SEQ], sps[:, 0, :]).then_inc(f_step, 1)
                nc.vector.tensor_copy(cum[:, TQ:TK], sps[:, 1, 0:PAST]).then_inc(f_step, 1)
                nc.vector.tensor_copy(cum[:, SEQ:TQ], sps[:, 1, PAST:PAST + P]).then_inc(f_step, 1)
                dve.wait_ge(cum_hi, 1)
                nc.vector.tensor_copy(aug_m[64:96, :], cumh[64:96, 0:TQ].bitcast(F32)).then_inc(f_step, 1)
                tt(aug_m[96:128, :], cum[96:128, 0:TQ], cumh[96:128, 0:TQ].bitcast(F32), ALU.subtract
                   ).then_inc(f_step, 1)
                nc.vector.tensor_scalar(aug_r[0:32, :], cumh[0:32, :].bitcast(F32), -1.0, None, ALU.mult
                                        ).then_inc(f_step, 1)
                tt(aug_r[32:64, :], cumh[32:64, :].bitcast(F32), cum[32:64, :], ALU.subtract).then_inc(f_step, 1)
                dve.wait_ge(f_step, 12)
                dve.wait_ge(aug_ones, 2)

            def clear_pads():
                for s in range(2):
                    nc.vector.memset(qh[s][:, T:TQ].bitcast(F32), 0.0).then_inc(pads_zero, 1)
                    nc.vector.memset(ql[s][:, T:TQ].bitcast(F32), 0.0).then_inc(pads_zero, 1)
                nc.vector.memset(kf[:, T:TQ], 0.0).then_inc(pads_zero, 1)
                nc.vector.memset(vf[:, T:TQ], 0.0).then_inc(pads_zero, 1)

            nc.vector.memset(eps[:, 0:1], EPS).then_inc(eps_set, 1)
            nc.vector.memset(eps[:, 1:2], SUB_EPS).then_inc(eps_set, 1)
            clear_pads()
            dve.wait_ge(small_loaded, 16)
            tt(og[:, 0:P], lam_p[:, 0:P], lam_p[:, P:2 * P], ALU.mult).then_inc(lam_step, 1)
            dve.wait_ge(lam_step, 1)
            nc.vector.tensor_reduce(nlam[:, 0:2], og[:, 0:P].rearrange("p (a b) -> p a b", a=2), AX_X, ALU.add
                                    ).then_inc(lam_step, 1)
            dve.wait_ge(w_hi_done, 1)
            tt(w_lo[0][:, 0:KT // 2, :], w_raw[0][:, 0:KT // 2, :], w_hi[0][:, 0:KT // 2, :].bitcast(F32),
               ALU.subtract).then_inc(w_lo_first, 1)

            def add_square(k):
                dve.wait_ge(sq_act, (k + 1) // 2 if k < 6 else k - 2)
                dve.wait_ge(sq_pool, min(k // 2, 2) + 1)
                if k == 1:
                    tt(acc[:], sq_all[:, 0, :], sq_all[:, 1, :], ALU.add).then_inc(acc_done, 2)
                else:
                    dve.wait_ge(acc_done, k)
                    tt(acc[:], acc[:], sq_all[:, k, :], ALU.add).then_inc(acc_done, 1)

            for k in range(KT):
                dve.wait_ge(xh_done, k + 1)
                stt(xl[:, k, :], xT[:, k, :], norm_w[0][:, k:k + 1], xh[:, k, :].bitcast(F32), ALU.mult, ALU.subtract
                    ).then_inc(xl_done, 1)
                if k >= 3:
                    add_square(k - 2)
            add_square(KT - 2)
            add_square(KT - 1)
            dve.wait_ge(lam_exp, 1)
            tt(nlam[:, 4:5], nlam[:, 3:4], nlam[:, 2:3], ALU.subtract).then_inc(lam_step, 1)
            dve.wait_ge(lam_step, 3)
            nc.vector.tensor_scalar(nlam[:, 5:6], nlam[:, 4:5], -LAM_INIT, None, ALU.add).then_inc(lam_step, 1)
            nc.vector.tensor_scalar(sub_w[:], subln, 1.0 - LAM_INIT, None, ALU.mult).then_inc(on_done, 1)
            dve.wait_ge(rope_loaded, 32)
            dve.wait_ge(r_ready, 1)
            dve.wait_ge(lam_step, 4)
            dve.wait_ge(on_done, 1)
            tt(cosr[:], cosr[:], rs[:], ALU.mult).then_inc(rope_scaled, 1)
            tt(sinr[:], sinr[:], rs[:], ALU.mult).then_inc(rope_scaled, 1)
            dve.wait_ge(rope_scaled, 2)
            for L in (DIFF, FOX):
                if L == FOX:
                    clear_pads()
                    dve.wait_ge(r_ready, 3)
                group(L, Num(0), 0, alone=True)
                group(L, Num(1), 1, first=True)
                with dve.Fori(0, 3) as it:
                    for par in range(2):
                        group(L, Num(2 + par, 2, it), par)

                def wo_residual(j):
                    if j < WO_EARLY:
                        dve.wait_ge(wo_done, WO_EARLY * L + j + 1)
                    else:
                        dve.wait_ge(w_used, U_LAYER * L + U_WO + (WO_END[j] + 1) // KT)
                    residual(Num(N_LAYER * L + N_WO + j), Num(WO_STEPS[WO_END[j]][1]))

                for slot in range(SLOTS):
                    for j in range(3):
                        if WO_END[j] + 1 == slot:
                            wo_residual(j)
                    attention(L, Num(7), 1, slot)
                wo_residual(3)
                if L == DIFF:
                    norm_o(Num(7))
                    split_o(Num(7))
                else:
                    o_lo(Num(7), 1)
                clear_acc(2 * L + 1)
                for j in range(4, 10):
                    wo_residual(j)
                for k in range(6):
                    prep(2 * L + 1, Num(k))
                for k in (6, 7):
                    wo_residual(4 + k)
                    prep(2 * L + 1, Num(k))
                dve.wait_ge(r_ready, val(2 * L + 2))

                def gate_up(jt):
                    j = jt + FT * L
                    u, n = jt * 2 + (U_LAYER * L + U_IN), jt * 2 + (N_LAYER * L + N_IN)
                    if some(j):
                        dve.wait_ge(sg_done, val(j))
                    take(gf[:], u + 1, n, rs[:])
                    if some(j):
                        dve.wait_ge(hf_done, val(j))
                    take(uf[:], u + 2, n + 1, rs[:])
                    dve.wait_ge(hh_done, val(j + 1))
                    tt(at(hl, jt), hf[:], at(hh, jt).bitcast(F32), ALU.subtract).then_inc(hl_done, 1)

                gate_up(Num(0))
                with dve.Fori(0, FT - 1) as it:
                    gate_up(Num(1, 1, it))
                clear_acc(2 * L + 2)
                with dve.Fori(0, KT // 2) as it:
                    for s in range(2):
                        k = Num(s, 2, it)
                        dve.wait_ge(w_used, val(Num(U_LAYER * L + U_OUT + 3 * (s + 1), 6, it)))
                        residual(k + (N_LAYER * L + N_OUT), k)
                        prep(2 * L + 2, k)
            dve.wait_ge(r_ready, 5)
            for k in range(KT):
                stt(yt[:, k, :], xT[:, k, :], norm_w[4][:, k:k + 1], rs[:], ALU.mult, ALU.mult).then_inc(y_done, 1)


def at_cols(tile, i, rows, cols):
    if i.it is None or i.k == 0:
        return tile[rows, i.c, cols]
    return tile[rows, bass.ds(i.v(), 1), cols].rearrange("p a b -> p (a b)")


def kernel(**inputs):
    import numpy as np
    import ml_dtypes
    import concourse.bacc as bacc
    from concourse.bass_utils import run_bass_kernel_spmd as run

    a = {k: np.asarray(v) for k, v in inputs.items()}

    def units(w):
        k, n = w.shape
        return w.reshape(k // P, P, n // P, P).transpose(2, 1, 0, 3).reshape(n // P, P, k)

    def pad(w, width_):
        out = np.zeros(w.shape[:-1] + (width_,), w.dtype)
        out[..., :w.shape[-1]] = w
        return out

    stream = []
    for L, (w_in, w_o) in enumerate(((a["diff_w_qkv"][0], a["diff_w_o"][0]), (a["fox_w_qkvf"][0], a["fox_w_o"][0]))):
        q, k, v = (units(w_in[:, i * D:(i + 1) * D]) for i in range(3))
        stream += [x for g in range(G) for x in (k[g:g + 1], q[g:g + 1], v[g:g + 1])]
        blocks = units(w_o).reshape(KT, P, KT, P)
        stream.append(np.stack([blocks[tile, :, k] for _, tile, k in WO_STEPS])
                      .reshape(KT, KT, P, P).transpose(0, 2, 1, 3).reshape(KT, P, D))
        gate, up = units(a["ffn_w_in"][L][:, :F]), units(a["ffn_w_in"][L][:, F:])
        stream.append(np.stack([gate, up], 1).reshape(2 * FT, P, D))
        out = units(a["ffn_w_out"][L])
        stream.append(pad(out, 3 * D).reshape(KT, P, 3, D).transpose(0, 2, 1, 3).reshape(3 * KT, P, D))
    w_units = np.concatenate(stream)

    def quadrants(x):
        out = np.zeros(x.shape[:-1] + (4, 32), x.dtype)
        out[..., :, :2 * G] = x[..., None, :]
        return out.reshape(x.shape[:-1] + (P,))

    w_forget = units(quadrants(a["fox_w_qkvf"][0][:, 3 * D:]))[0]
    x_in = np.concatenate([a["x_prompt"][0], a["x_sample"][0]]).T
    cols = [a[n][i].reshape(KT, P).T for i in range(2) for n in ("norm_mix", "norm_ffn")]
    lam = a["diff_lambda"][0]
    small = np.concatenate(
        cols + [a["norm_final"].reshape(KT, P).T, a["diff_subln"][0][:, None], quadrants(a["fox_b_f"][0])[:, None],
                np.broadcast_to(lam[[0, 2, 1, 3]].reshape(1, 2 * P), (P, 2 * P))], 1)
    tri = np.triu(np.ones((P, P), np.float32))
    sel = quadrants(np.eye(2 * G, dtype=np.float32)).T
    cst = np.concatenate([np.eye(P, dtype=np.float32), np.ones((P, P), np.float32), sel,
                          tri, np.ones((P, SEQ - P), np.float32)], 1)
    chunk = np.arange(P) // 64
    masked = np.float32(-1e30)
    cst16 = np.concatenate([np.eye(P), np.where(chunk[None] <= chunk[:, None], 0, masked),
                            np.where(np.arange(P)[None] <= np.arange(P)[:, None], 0, masked)], 1
                           ).astype(ml_dtypes.bfloat16)
    pos = np.concatenate([np.arange(SEQ), PAST + np.arange(NEW)]).astype(np.float32)
    freq = (10000.0 ** -(np.arange(32) / 32)).astype(np.float32)
    ang = freq[:, None] * pos[None]
    cos, sin = np.cos(ang), np.sin(ang)
    rope_tab = np.concatenate([np.tile(cos, (4, 1)), np.concatenate([-sin, sin, -sin, sin])], 1)
    k_past = np.concatenate([a["cache_diff_k"][0, 0].reshape(PAST, D).T, a["cache_fox_k"][0, 0].reshape(PAST, D).T])

    def frames(x):
        return x.reshape(2, P, -1, P).transpose(2, 1, 0, 3).reshape(-1, P, 2 * P)

    v_past = np.concatenate([frames(a["cache_diff_v"][0, 0].reshape(PAST, D)),
                             frames(a["cache_fox_v"][0, 0].reshape(PAST, D))])
    f_past = frames(quadrants(a["cache_fox_logf"][0, 0]))[0]

    nc = bacc.Bacc("TRN2", target_bir_lowering=False, num_devices=1)
    arrays, args = {}, []
    for name, x in (("w_units", w_units), ("w_forget", w_forget), ("x_in", x_in), ("small", small), ("cst", cst),
                    ("cst16", cst16), ("rope_tab", rope_tab), ("k_past", k_past), ("v_past", v_past),
                    ("f_past", f_past)):
        x = np.ascontiguousarray(x)
        arrays[name] = x
        args.append(nc.dram_tensor(name, x.shape, mybir.dt.from_np(x.dtype), kind="ExternalInput").ap())
    outs = (("y_out", D), ("dk_out", D), ("dv_out", D), ("fk_out", D), ("fv_out", D), ("lf_out", 2 * G))
    for name, rows in outs:
        args.append(nc.dram_tensor(name, (rows, T), F32, kind="ExternalOutput").ap())
    encoder(nc, *args)
    got = run(nc, [arrays], core_ids=[0]).results[0]
    y, dk, dv, fk, fv, lf = (np.ascontiguousarray(got[name].T) for name, _ in outs)

    def part(x, s, shape):
        x = x[:SEQ] if s == 0 else x[SEQ:]
        return x.reshape(shape[:2] + (x.shape[0],) + shape[2:])

    res = [y[:SEQ].reshape(1, SEQ, D), y[SEQ:].reshape(1, NEW, D)]
    for s in range(2):
        res += [part(dk, s, (1, 1, 16, 64)), part(dv, s, (1, 1, 8, 128)), part(fk, s, (1, 1, 16, 64)),
                part(fv, s, (1, 1, 16, 64)), part(lf, s, (1, 1, 16))]
    return tuple(res)
```
